# Optimizing a Trainium2 kernel written in Bass

```python
import jax, jax.numpy as jnp
from jax import lax
import numpy as np

D_MODEL = 2048
BATCH = 1
SEQ = 512
DEPTH = 1

P_DIM = 256
CHUNK = 64
MIX_WIDTH = D_MODEL
MLSTM_WIDTH = MIX_WIDTH // 2
MLSTM_HEADS = 8
MLSTM_HEAD_DIM = MLSTM_WIDTH // MLSTM_HEADS
QK_CONV = 4
POOL_WIDTH = MIX_WIDTH - MLSTM_WIDTH
POOL_WINDOWS = (2, 4, 8, 16)
POOL_GROUPS = len(POOL_WINDOWS)
POOL_GROUP_WIDTH = POOL_WIDTH // POOL_GROUPS
D_FF = 4 * D_MODEL
IN_COLS = 4 * MLSTM_WIDTH + 2 * MLSTM_HEADS + POOL_WIDTH
SPLITS = [MLSTM_WIDTH, 2 * MLSTM_WIDTH, 3 * MLSTM_WIDTH, 4 * MLSTM_WIDTH,
          4 * MLSTM_WIDTH + MLSTM_HEADS, 4 * MLSTM_WIDTH + 2 * MLSTM_HEADS]
EPS = 1e-6

kernel_name = "hybrid_mlstm_pool_stream_block"

def rms_norm(x, g):
    xf = x.astype(jnp.float32)
    y = xf * lax.rsqrt(jnp.mean(xf * xf, axis=-1, keepdims=True) + EPS)
    return (y * g.astype(jnp.float32)).astype(x.dtype)

def causal_depthwise_conv(x, w):
    K = w.shape[0]
    S = x.shape[1]
    xp = jnp.pad(x, ((0, 0), (K - 1, 0), (0, 0)))
    y = xp[:, 0:S] * w[0]
    for k in range(1, K):
        y = y + xp[:, k:k + S] * w[k]
    return y

def mlstm_chunkwise(q, k, v, log_i, log_f):
    B, S, H, Dh = q.shape
    L = CHUNK
    NC = S // L

    def to_chunks(t):
        t = t.reshape((B, NC, L, H) + t.shape[3:])
        return jnp.moveaxis(t, 3, 1)

    qc = to_chunks(q)
    kc = to_chunks(k) * (Dh ** -0.5)
    vc = to_chunks(v)
    li = to_chunks(log_i)
    lf = to_chunks(log_f)
    b = jnp.cumsum(lf, axis=-1)
    b_tot = b[..., -1]
    a = b_tot[..., None] - b + li
    a_max = jnp.max(a, axis=-1)

    def step(carry, xs):
        C, n, m = carry
        k_c, v_c, a_c, amax_c, btot_c = xs
        m_new = jnp.maximum(btot_c + m, amax_c)
        decay = jnp.exp(btot_c + m - m_new)
        w = jnp.exp(a_c - m_new[..., None])
        C_new = decay[..., None, None] * C + jnp.einsum('bhl,bhld,bhle->bhde', w, v_c, k_c)
        n_new = decay[..., None] * n + jnp.einsum('bhl,bhle->bhe', w, k_c)
        return (C_new, n_new, m_new), (C, n, m)

    xs = (jnp.moveaxis(kc, 2, 0), jnp.moveaxis(vc, 2, 0), jnp.moveaxis(a, 2, 0),
          jnp.moveaxis(a_max, 2, 0), jnp.moveaxis(b_tot, 2, 0))
    init = (jnp.zeros((B, H, Dh, Dh), jnp.float32),
            jnp.zeros((B, H, Dh), jnp.float32),
            jnp.zeros((B, H), jnp.float32))
    _, (C_prev, n_prev, m_prev) = lax.scan(step, init, xs)
    C_prev = jnp.moveaxis(C_prev, 0, 2)
    n_prev = jnp.moveaxis(n_prev, 0, 2)
    m_prev = jnp.moveaxis(m_prev, 0, 2)

    inter_log = b + m_prev[..., None]
    causal = jnp.tril(jnp.ones((L, L), dtype=bool))
    Dlog = b[..., :, None] - b[..., None, :] + li[..., None, :]
    Dlog = jnp.where(causal, Dlog, -jnp.inf)
    m_t = jnp.maximum(inter_log, jnp.max(Dlog, axis=-1))
    Dw = jnp.exp(Dlog - m_t[..., None])
    inter_w = jnp.exp(inter_log - m_t)
    s = jnp.einsum('bhcld,bhcjd->bhclj', qc, kc) * Dw
    num = (inter_w[..., None] * jnp.einsum('bhcde,bhcle->bhcld', C_prev, qc)
           + jnp.einsum('bhclj,bhcjd->bhcld', s, vc))
    den = inter_w * jnp.einsum('bhce,bhcle->bhcl', n_prev, qc) + jnp.sum(s, axis=-1)
    h = num / jnp.maximum(jnp.abs(den), jnp.exp(-m_t))[..., None]
    return jnp.moveaxis(h, 1, 3).reshape(B, S, H, Dh)

def multiscale_pool(u, w_pool, scale):
    B, S, _ = u.shape
    uf = u.astype(jnp.float32)
    cs = jnp.pad(jnp.cumsum(uf, axis=1), ((0, 0), (1, 0), (0, 0)))
    t1 = jnp.arange(1, S + 1, dtype=jnp.float32)
    outs = []
    for g, w in enumerate(POOL_WINDOWS):
        sl = slice(g * POOL_GROUP_WIDTH, (g + 1) * POOL_GROUP_WIDTH)
        hi = cs[:, 1:, sl]
        lo = jnp.pad(cs[:, :S + 1 - w, sl], ((0, 0), (w - 1, 0), (0, 0)))
        mean = (hi - lo) / jnp.minimum(t1, w)[None, :, None]
        outs.append(mean - uf[..., sl])
    pooled = jnp.stack(outs, axis=2).astype(u.dtype)
    mixed = jnp.einsum('bsgc,gcd->bsgd', pooled, w_pool)
    return mixed.reshape(B, S, POOL_WIDTH) * scale

def setup_inputs(seed: int = 0) -> dict:
    key = jax.random.key(seed)
    ks = jax.random.split(key, 24)
    H = MLSTM_HEADS
    nrm = lambda k, shape, s: jax.random.normal(k, shape, jnp.float32) * s
    gain = lambda k, shape: 1.0 + 0.05 * jax.random.normal(k, shape, jnp.float32)
    f_bias = jnp.linspace(3.0, 6.0, H, dtype=jnp.float32)
    b_gates = jnp.concatenate([
        nrm(ks[3], (DEPTH, H), 0.1),
        f_bias[None, :] + nrm(ks[4], (DEPTH, H), 0.1)], axis=-1)
    return {
        "x": nrm(ks[0], (BATCH, SEQ, D_MODEL), 1.0),
        "p": nrm(ks[1], (DEPTH, BATCH, SEQ, P_DIM), 1.0),
        "w_in": nrm(ks[2], (DEPTH, D_MODEL, IN_COLS), D_MODEL ** -0.5),
        "b_gates": b_gates,
        "w_qk_conv": nrm(ks[5], (DEPTH, QK_CONV, 2 * MLSTM_WIDTH), QK_CONV ** -0.5),
        "g_mlstm": gain(ks[6], (DEPTH, MLSTM_WIDTH)),
        "w_pool": nrm(ks[7], (DEPTH, POOL_GROUPS, POOL_GROUP_WIDTH, POOL_GROUP_WIDTH), POOL_GROUP_WIDTH ** -0.5),
        "pool_scale": gain(ks[8], (DEPTH, POOL_WIDTH)),
        "w_out": nrm(ks[9], (DEPTH, MIX_WIDTH, D_MODEL), MIX_WIDTH ** -0.5),
        "g_mix_pre": gain(ks[10], (DEPTH, D_MODEL)),
        "g_mix_post": gain(ks[11], (DEPTH, D_MODEL)),
        "w_ff1": nrm(ks[12], (DEPTH, D_MODEL, D_FF), D_MODEL ** -0.5),
        "w_ff2": nrm(ks[13], (DEPTH, D_FF, D_MODEL), D_FF ** -0.5),
        "g_ff_pre": gain(ks[14], (DEPTH, D_MODEL)),
        "g_ff_post": gain(ks[15], (DEPTH, D_MODEL)),
        "w_ple_proj": nrm(ks[16], (DEPTH, P_DIM, D_MODEL), P_DIM ** -0.5),
        "w_ple_gate": nrm(ks[17], (DEPTH, D_MODEL, D_MODEL), D_MODEL ** -0.5),
        "g_ple_gate": gain(ks[18], (DEPTH, D_MODEL)),
        "g_ple_post": gain(ks[19], (DEPTH, D_MODEL)),
    }

def reference(x, p, w_in, b_gates, w_qk_conv, g_mlstm, w_pool, pool_scale, w_out,
              g_mix_pre, g_mix_post, w_ff1, w_ff2, g_ff_pre, g_ff_post,
              w_ple_proj, w_ple_gate, g_ple_gate, g_ple_post):
    B, S, _ = x.shape
    H, Dh = MLSTM_HEADS, MLSTM_HEAD_DIM
    h = x
    for i in range(DEPTH):
        xn = rms_norm(h, g_mix_pre[i])
        proj = xn @ w_in[i]
        q, k, v, o, gi, gf, u = jnp.split(proj, SPLITS, axis=-1)
        qk = jax.nn.silu(causal_depthwise_conv(jnp.concatenate([q, k], axis=-1), w_qk_conv[i]))
        q, k = jnp.split(qk, 2, axis=-1)
        gates = jnp.concatenate([gi, gf], axis=-1).astype(jnp.float32) + b_gates[i].astype(jnp.float32)
        log_i = gates[..., :H]
        log_f = jax.nn.log_sigmoid(gates[..., H:])
        cell = mlstm_chunkwise(q.reshape(B, S, H, Dh).astype(jnp.float32),
                               k.reshape(B, S, H, Dh).astype(jnp.float32),
                               v.reshape(B, S, H, Dh).astype(jnp.float32),
                               log_i, log_f).astype(x.dtype)
        cell = rms_norm(cell, g_mlstm[i].reshape(H, Dh))
        h_ml = (jax.nn.sigmoid(o).reshape(B, S, H, Dh) * cell).reshape(B, S, MLSTM_WIDTH)
        h_pool = multiscale_pool(u, w_pool[i], pool_scale[i])
        mix = jnp.concatenate([h_ml, h_pool], axis=-1) @ w_out[i]
        h = h + rms_norm(mix, g_mix_post[i])
        hn = rms_norm(h, g_ff_pre[i])
        ff = jnp.square(jax.nn.relu(hn @ w_ff1[i])) @ w_ff2[i]
        h = h + rms_norm(ff, g_ff_post[i])
        gate = jax.nn.sigmoid(rms_norm(h, g_ple_gate[i]) @ w_ple_gate[i])
        e = p[i] @ w_ple_proj[i]
        h = h + rms_norm(e * gate, g_ple_post[i])
    return h


_drawn_inputs = setup_inputs


def setup_inputs(seed=0):
    import zlib

    import numpy as np

    out = dict(_drawn_inputs(seed))
    spreads = {}
    factors = {'g_mlstm': 3.085, 'g_ple_gate': 5.804}
    for name, (base, spread) in spreads.items():
        noise = np.random.default_rng([zlib.crc32(name.encode()), seed]).standard_normal(out[name].shape)
        drawn = base * np.exp(spread * noise) if base else spread * noise
        out[name] = __import__('jax').numpy.asarray(drawn.astype(out[name].dtype))
    for name, factor in factors.items():
        out[name] = (out[name] * factor).astype(out[name].dtype)
    return out
```

```python
from contextlib import ExitStack

import concourse.bass as bass
from concourse import mybir

F32 = mybir.dt.float32
F32R = mybir.dt.float32r
ALU = mybir.AluOpType
ACT = mybir.ActivationFunctionType

P = 128
S = 512
D = 2048
KT = D // P
H = 8
HH = H // 2
TT = S // P
NT = 4
CONV = 4
WINDOWS = (2, 4, 8, 16)
EPS = 1e-6
FF = 4 * D
CHUNKS = 8
HT = FF // CHUNKS // P
DEPTH = 4
LEAD = DEPTH - 1

U_V0 = 0
U_GATES = U_V0 + 8
U_O0 = U_GATES + 1
U_Q0 = U_O0 + 8
U_K0 = U_Q0 + 8
U_O1 = U_K0 + 8
U_V1 = U_O1 + 8
U_Q1 = U_V1 + 8
U_K1 = U_Q1 + 8
U_U0 = U_K1 + 8
U_U1 = U_U0 + 8
U_POOL0 = U_U1 + 8
U_OUT0A = U_POOL0 + 1
U_POOL1 = U_OUT0A + 4
U_OUT0B = U_POOL1 + 1
U_OUT1 = U_OUT0B + 4
U_FF = U_OUT1 + 24
FF_UNITS = 32
U_P = U_FF + CHUNKS * FF_UNITS
U_PLE = U_P + 1
U_GATE = U_PLE + 4
UNITS = U_GATE + 32

(G_V0, G_O0, G_Q0, G_K0, G_O1, G_V1, G_Q1, G_K1, G_U0, G_U1, G_POOL0, G_POOL1, G_OUT) = range(13)
G_FF = G_OUT + 4
G_PLE = G_FF + 6 * CHUNKS
G_GATE = G_PLE + 4

C_MIX_PRE, C_MIX_POST, C_FF_PRE, C_FF_POST, C_PLE_GATE, C_PLE_POST = (KT * i for i in range(6))
C_MLSTM = 6 * KT
C_POOL = C_MLSTM + H
C_CONV = C_POOL + 8
C_BIAS = C_CONV + 16 * CONV
PARAMS = C_BIAS + 2

OFF = [(0, 1), (0, 2), (0, 3), (1, 2), (1, 3), (2, 3)]
BLOCK = {(j, j): j for j in range(TT)} | {jt: TT + i for i, jt in enumerate(OFF)}
BLOCKS = len(BLOCK)
NEG = -1e30
XL_MIX = KT
XL_FF = XL_MIX + H
XL_GATE = XL_FF + KT
EXP_MAX = 88.0


def banks_of(g):
    if g in (G_POOL0, G_POOL1):
        return 4
    if g < G_OUT or G_PLE <= g < G_GATE:
        return 0
    if g >= G_GATE:
        return 4 * ((g - G_GATE + 1) % 2)
    return 4 * ((g - G_OUT) % 2)


def build(nc, stream, x_t, params, out_t):
    ctx = ExitStack()
    with ctx:
        def sem(name):
            return ctx.enter_context(nc.semaphore(name))

        def sb(name, shape, dt=F32, stack=ctx):
            return stack.enter_context(nc.sbuf_tensor(name, shape, dt))

        hb = sb("hb", [P, KT, S])
        xh = sb("xh", [P, KT, S], F32R)
        xl = sb("xl", [P, KT, S], F32R)
        raw = sb("raw", [P, DEPTH, 1024])
        wh = sb("wh", [P, DEPTH, 1024], F32R)
        wl = sb("wl", [P, DEPTH, 1024], F32R)
        tmp = sb("tmp", [P, 2, S])
        row = sb("row", [P, S])
        ssq = sb("ssq", [P, S])
        ident = sb("ident", [P, P])
        ones = sb("ones", [P, P])
        mask = sb("mask", [P, P])
        par = sb("par", [P, PARAMS])
        eps = sb("eps", [P, 1])
        win = sb("win", [P, 16])
        tokf = sb("tokf", [P, TT])
        gsb = sb("gsb", [P, TT, 2 * H])
        colt = sb("colt", [P, BLOCKS + TT, H])
        mp = sb("mp", [H, TT])
        nsel = sb("nsel", [H, 2, P])
        den = sb("den", [P, TT])
        cssq = sb("cssq", [P, TT])
        crs = sb("crs", [P, TT])
        mixer = ExitStack()
        with mixer:
            vh = sb("vh", [P, TT, HH, 130], F32R, mixer)
            vl = sb("vl", [P, TT, HH, 130], F32R, mixer)
            qh = sb("qh", [P, HH, S], F32R, mixer)
            ql = sb("ql", [P, HH, S], F32R, mixer)
            kh = sb("kh", [P, HH, S], F32R, mixer)
            kl = sb("kl", [P, HH, S], F32R, mixer)
            dw = sb("dw", [P, BLOCKS * P], F32, mixer)
            ph = sb("ph", [P, BLOCKS * P], F32R, mixer)
            pl = sb("pl", [P, BLOCKS * P], F32R, mixer)
        acc = sb("acc", [P, KT, S])
        hid_stack = ExitStack()
        with hid_stack:
            hidh = sb("hidh", [P, HT, S], F32R, hid_stack)
            hidl = sb("hidl", [P, HT, S], F32R, hid_stack)
        emb = sb("emb", [P, KT, S])
        ssq2 = sb("ssq2", [P, S])
        ml = ssq[0:H, :]
        cn = tmp[:, 0, :]

        bank = [ctx.enter_context(nc.psum_tensor(f"bank{i}", [P, 512], F32)) for i in range(8)]

        x_in = [sem(f"x_in{j}") for j in range(KT // 2)]
        par_in = sem("par_in")
        xr_in = sem("xr_in")
        raw_in = [sem(f"raw_in{s}") for s in range(DEPTH)]
        hi_ready = sem("hi_ready")
        lo_ready = sem("lo_ready")
        pieces = sem("pieces")
        tile_read = sem("tile_read")
        consts = sem("consts")
        xh_ready = sem("xh_ready")
        xl_ready = sem("xl_ready")
        sq_ready = sem("sq_ready")
        ss_ready = sem("ss_ready")
        stat_mm = sem("stat_mm")
        row_ready = sem("row_ready")
        vh_ready = sem("vh_ready")
        g_mm = sem("g_mm")
        g_sb = sem("g_sb")
        g_tr = sem("g_tr")
        g_ln = sem("g_ln")
        g_x = sem("g_x")
        c_sb = sem("c_sb")
        c_tr = sem("c_tr")
        c_ready = sem("c_ready")
        em_ready = sem("em_ready")
        sig_ready = sem("sig_ready")
        y_ready = sem("y_ready")
        qk_f = sem("qk_f")
        qk_h = sem("qk_h")
        qk_l = sem("qk_l")
        sel_ready = sem("sel_ready")
        r_mm = sem("r_mm")
        diag_ready = sem("diag_ready")
        d_ready = sem("d_ready")
        s_mm = sem("s_mm")
        p_f = sem("p_f")
        p_h = sem("p_h")
        p_l = sem("p_l")
        n_mm = sem("n_mm")
        n_read = sem("n_read")
        cs_ready = sem("cs_ready")
        cr_ready = sem("cr_ready")
        cn_ready = sem("cn_ready")
        tr_mm = sem("tr_mm")
        cell_ready = sem("cell_ready")
        pool_f = sem("pool_f")
        pool_h = sem("pool_h")
        pool_l = sem("pool_l")
        h_ready = sem("h_ready")
        hid_h = sem("hid_h")
        hid_l = sem("hid_l")
        ff_sq = sem("ff_sq")
        p_copied = sem("p_copied")
        ffrow = sem("ffrow")
        ffrow_v = sem("ffrow_v")
        gsig = sem("gsig")
        prod_ready = sem("prod_ready")
        fin_g = sem("fin_g")
        dve_chain = sem("dve_chain")
        act_chain = sem("act_chain")
        pool_chain = sem("pool_chain")
        out_v = sem("out_v")
        out_g = sem("out_g")
        stored = sem("stored")

        block = ctx.enter_context(nc.Block())

        def linker(eng, chain):
            count = [0]

            def link(*instructions):
                for ins in instructions:
                    ins.then_inc(chain, 1)
                count[0] += len(instructions)
                eng.wait_ge(chain, count[0])
            return link

        def g(col, kt):
            return par[:, col + kt:col + kt + 1]

        @block.sync
        def _(sp):
            def load(u, first=False):
                sp.dma_start(raw[:, u % DEPTH, :], stream[u]).then_inc(raw_in[u % DEPTH], 16)

            xv = x_t.rearrange("(j k p) t -> j p k t", k=2, p=P)
            for j in range(KT // 2):
                sp.dma_start(hb[:, 2 * j:2 * j + 2, :], xv[j]).then_inc(x_in[j], 16)
                if j < DEPTH:
                    load(j)
                if j == 0:
                    sp.dma_start(par[:, :], params).then_inc(par_in, 16)

            def load_loop(lo, hi):
                with sp.Fori(lo, hi) as i:
                    for s in range(DEPTH):
                        sp.wait_ge(lo_ready, DEPTH * i + (s + 1 - DEPTH))
                        src = stream[bass.ds(DEPTH * i + s, 1)].rearrange("o p n -> p (o n)")
                        sp.dma_start(raw[:, s, :], src).then_inc(raw_in[s], 16)

            turn = (U_OUT1 + 12) // DEPTH
            load_loop(1, turn)
            sp.wait_ge(xl_ready, XL_MIX + H)
            sp.wait_ge(pool_l, 2 * NT)
            for j in range(KT // 2):
                sp.dma_start(hb[:, 2 * j:2 * j + 2, :], xv[j]).then_inc(xr_in, 16)
            load_loop(turn, UNITS // DEPTH)
            ov = out_t.rearrange("(k p) t -> k p t", p=P)
            for m in VECTOR_TILES:
                sp.wait_ge(out_v, VECTOR_TILES.index(m) + 1)
                sp.dma_start(ov[m], hb[:, m, :]).then_inc(stored, 16)
            sp.wait_ge(stored, 16 * KT)

        @block.gpsimd
        def _(pool):
            pool.memset(ones[:, :], 1.0).then_inc(consts, 1)
            pool.memset(eps[:, :], EPS).then_inc(consts, 1)
            pool.memset(ident[:, :], 1.0).then_inc(pool_chain, 1)
            pool.memset(mask[:, :], 0.0).then_inc(pool_chain, 1)
            pool.wait_ge(pool_chain, 2)
            pool.affine_select(out=ident[:, :], in_=ident[:, :], compare_op=ALU.is_equal, fill=0.0,
                               base=0, pattern=[[-1, P]], channel_multiplier=1).then_inc(consts, 1)
            pool.affine_select(out=mask[:, :], in_=mask[:, :], compare_op=ALU.is_ge, fill=NEG,
                               base=0, pattern=[[1, P]], channel_multiplier=-1).then_inc(consts, 1)
            with pool.Fori(0, UNITS // DEPTH) as i:
                for s in range(DEPTH):
                    pool.wait_ge(hi_ready, DEPTH * i + s + 1)
                    pool.tensor_tensor(wl[:, s, :], raw[:, s, :], wh[:, s, :].bitcast(F32),
                                       ALU.subtract).then_inc(lo_ready, 1)
            pool.wait_ge(row_ready, 4)
            for i, m in enumerate(POOL_TILES):
                pool.wait_ge(fin_g, m + 1)
                pool.tensor_tensor(acc[:, m, :], acc[:, m, :], row[:, :], ALU.mult).then_inc(pool_chain, 1)
                pool.wait_ge(pool_chain, 3 + i)
                pool.tensor_tensor(hb[:, m, :], hb[:, m, :], acc[:, m, :], ALU.add).then_inc(out_g, 1)

        @block.tensor
        def _(pe):
            held = {}

            def claim(g_, n):
                b = banks_of(g_) + n
                if b in held:
                    pe.wait_ge(tile_read, held[b] + 1)
                held[b] = NT * g_ + n
                return bank[b]

            def three(out, a, b, first, last):
                pe.matmul(out, a[0], b[0], start=first, stop=False)
                pe.matmul(out, a[0], b[1], start=False, stop=False)
                return pe.matmul(out, a[1], b[0], start=False, stop=last)

            def weights(u, k, c0, c1):
                s = u % DEPTH
                return (wh[:, s, S * k + c0:S * k + c1], wl[:, s, S * k + c0:S * k + c1])

            def unit(u, g_, rhs, kts, need=None, first=True, last=True, tokens_out=False, inc=1):
                pe.wait_ge(lo_ready, u + 1)
                if need:
                    pe.wait_ge(need[0], need[1] + kts[1] + 1)
                for n in range(NT):
                    out = claim(g_, n) if first else bank[banks_of(g_) + n]
                    for k, kt in enumerate(kts):
                        x = (rhs[0][:, kt, :], rhs[1][:, kt, :])
                        st, en = first and k == 0, last and k == 1
                        if tokens_out:
                            x = tuple(v[:, n * P:(n + 1) * P] for v in x)
                            mm = three(out[:, :], x, weights(u, k, 0, S), st, en)
                        else:
                            mm = three(out[:, :], weights(u, k, n * P, (n + 1) * P), x, st, en)
                    mm.then_inc(pieces, inc if n == 0 else 1)

            X = (xh, xl)

            def group(u0, g_, need=None, tokens_out=False, after=None):
                for j in range(KT // 2):
                    unit(u0 + j, g_, X, (2 * j, 2 * j + 1), need, j == 0, j == KT // 2 - 1, tokens_out)
                    if after and j in after:
                        after[j]()

            def stat(b, src, held_until=None):
                pe.matmul(bank[b][:, :], ones[:, :], src[:, :], start=True, stop=True).then_inc(stat_mm, 1)

            pe.wait_ge(consts, 4)
            for j in range(7):
                unit(U_V0 + j, G_V0, X, (2 * j, 2 * j + 1), (xl_ready, 0), j == 0, False, True)
            pe.wait_ge(ss_ready, KT)
            for t in range(TT):
                pe.matmul(bank[5][:, 2 * t:2 * t + 2], ssq[:, t * P:(t + 1) * P], ones[:, 0:2],
                          start=True, stop=True)
            stat(4, ssq)
            unit(U_V0 + 7, G_V0, X, (14, 15), (xl_ready, 0), False, True, True)

            pe.wait_ge(lo_ready, U_GATES + 1)
            s = U_GATES % DEPTH
            for t in range(TT):
                for kt in range(KT):
                    a = (xh[:, kt, t * P:(t + 1) * P], xl[:, kt, t * P:(t + 1) * P])
                    w = (wh[:, s, 2 * H * kt:2 * H * (kt + 1)], wl[:, s, 2 * H * kt:2 * H * (kt + 1)])
                    mm = three(bank[6][:, 2 * H * t:2 * H * (t + 1)], a, w, kt == 0, kt == KT - 1)
                if t < TT - 1:
                    mm.then_inc(pieces, 1)
            mm.then_inc(g_mm, 1)

            def gates_across():
                pe.wait_ge(g_sb, 1)
                pe.wait_ge(row_ready, 1)
                for b, c in ((7, 0), (5, H)):
                    for t in range(TT):
                        tr = pe.transpose(bank[b][0:H, t * P:(t + 1) * P], gsb[:, t, c:c + H], ident[:, :])
                tr.then_inc(g_tr, 1)

            def columns_across():
                pe.wait_ge(c_sb, 1)
                for i in range(BLOCKS + TT):
                    tr = pe.transpose(bank[6][:, H * i:H * (i + 1)], column_source(i), ident[0:H, 0:H])
                tr.then_inc(c_tr, 1)

            def column_source(i):
                if i < TT:
                    return tmp[0:H, 0, i * P:(i + 1) * P]
                if i < BLOCKS:
                    o = pair_at(i - TT)
                    return dw[0:H, o:o + P]
                return tmp[0:H, 1, (i - BLOCKS) * P:(i - BLOCKS + 1) * P]

            for j in range(8):
                unit(U_O0 + j, G_O0, X, (2 * j, 2 * j + 1), None, j == 0, j == 7, inc=2 if j == 0 else 1)
                if j == 1:
                    gates_across()
                if j == 5:
                    columns_across()
            group(U_Q0, G_Q0)
            group(U_K0, G_K0)

            def R(h):
                pe.wait_ge(sel_ready, h + 1)
                if h:
                    pe.wait_ge(d_ready, h)
                pe.matmul(bank[4][:, :], nsel[:, h % 2, :], ml, start=True, stop=True).then_inc(r_mm, 1)

            def scores(h):
                i, hl = h % HH, h % HH
                pe.wait_ge(qk_l, 8 * (h // HH + 1))
                if h:
                    pe.wait_ge(n_read, h)
                else:
                    pe.wait_ge(c_ready, 1)
                if h >= 2:
                    pe.wait_ge(cell_ready, h - (h % HH > 0))
                for j in range(TT):
                    k = (kh[:, hl, j * P:(j + 1) * P], kl[:, hl, j * P:(j + 1) * P])
                    q = (qh[:, hl, j * P:(j + 1) * P], ql[:, hl, j * P:(j + 1) * P])
                    mm = three(bank[5][:, j * P:(j + 1) * P], k, q, True, True)
                mm.then_inc(s_mm, 1)
                for j, b, c in ((0, 6, 0), (1, 7, 0), (2, 7, 2 * P)):
                    n = (TT - 1 - j) * P
                    k = (kh[:, hl, j * P:(j + 1) * P], kl[:, hl, j * P:(j + 1) * P])
                    q = (qh[:, hl, (j + 1) * P:S], ql[:, hl, (j + 1) * P:S])
                    mm = three(bank[b][:, c:c + n], k, q, True, True)
                    if j != 1:
                        mm.then_inc(s_mm, 1)

            def cells(h):
                pe.wait_ge(p_l, 3 * (h + 1))
                if h % HH == 0:
                    pe.wait_ge(tile_read, NT * ((G_V1 if h else G_V0) + 1))
                for t in range(TT):
                    out = bank[5][:, 130 * t:130 * (t + 1)] if t < 3 else bank[6][:, 0:130]
                    for j in range(t + 1):
                        o = BLOCK[j, t] * P
                        mm = three(out, (ph[:, o:o + P], pl[:, o:o + P]),
                                   (vh[:, j, h % HH, :], vl[:, j, h % HH, :]), j == 0, j == t)
                mm.then_inc(n_mm, 1)

            def turn(h):
                pe.wait_ge(cn_ready, h + 1)
                pe.wait_ge(p_f, 3 * min(h + 2, HH * (h // HH + 1)))
                for t in range(TT):
                    tr = pe.transpose(bank[7][:, t * P:(t + 1) * P], cn[:, t * P:(t + 1) * P], ident[:, :])
                tr.then_inc(tr_mm, 1)

            def half(b, h0, u1, g1, u2, g2, tokens_out):
                steps = {2: lambda: R(h0)}
                for i in range(HH):
                    steps[3 + 2 * i] = lambda h=h0 + i, more=i + 1 < HH: (scores(h), R(h + 1) if more else None)
                    steps[4 + 2 * i] = lambda h=h0 + i, t=i > 0: (turn(h - 1) if t else None, cells(h))
                steps[4 + 2 * HH] = lambda: turn(h0 + HH - 1)
                group(u1, g1, after={j: f for j, f in steps.items() if j < 8})
                group(u2, g2, tokens_out=tokens_out, after={j - 8: f for j, f in steps.items() if j >= 8})

            half(0, 0, U_O1, G_O1, U_V1, G_V1, True)
            group(U_Q1, G_Q1)
            group(U_K1, G_K1)
            half(1, HH, U_U0, G_U0, U_U1, G_U1, False)

            def pool_unit(u, g_, src, need):
                pe.wait_ge(lo_ready, u + 1)
                pe.wait_ge(pool_l, need)
                s = u % DEPTH
                for n in range(NT):
                    out = claim(g_, n)
                    for k in range(2):
                        c = 512 * (n // 2) + 256 * k + P * (n % 2)
                        kt = 2 * (n // 2) + k
                        mm = three(out[:, :], (wh[:, s, c:c + P], wl[:, s, c:c + P]),
                                   (src[0][:, kt, :], src[1][:, kt, :]), k == 0, k == 1)
                    mm.then_inc(pieces, 1)

            pe.wait_ge(cell_ready, H)
            pool_unit(U_POOL0, G_POOL0, (qh, ql), NT)
            need = (xl_ready, XL_MIX)
            pooled = (tile_read, NT * G_POOL0 - H)
            for j in range(4):
                unit(U_OUT0A + j, G_OUT, X, (2 * j, 2 * j + 1), need, j == 0, False)
            pool_unit(U_POOL1, G_POOL1, (kh, kl), 2 * NT)
            for j in range(4):
                unit(U_OUT0B + j, G_OUT, X, (8 + 2 * j, 9 + 2 * j), pooled, False, j == 3)
            for i in range(3):
                group(U_OUT1 + 8 * i, G_OUT + 1 + i)
            pe.wait_ge(tile_read, NT * (G_OUT + 3))
            pe.wait_ge(ss_ready, 2 * KT)
            stat(3, ssq)
            pe.wait_ge(row_ready, 2)

            with pe.Fori(0, CHUNKS) as c:
                for k in range(2 + NT):
                    for j in range(8 if k < 2 else 4):
                        l = 8 * k + j if k < 2 else 16 + 4 * (k - 2) + j
                        s = (U_FF + l) % DEPTH
                        last = j == (7 if k < 2 else 3)
                        pe.wait_ge(lo_ready, FF_UNITS * c + (U_FF + l + 1))
                        if k < 2:
                            src, need_ = X, (xl_ready, XL_FF + 2 * j + 2)
                        else:
                            src, need_ = (hidh, hidl), (hid_l, HT * c + (2 * j + 2))
                        pe.wait_ge(*need_)
                        b = banks_of(G_FF + k)
                        for n in range(NT):
                            if j == 0:
                                pe.wait_ge(tile_read, NT * 6 * c + (NT * (G_FF + k - 2) + n + 1))
                            for kk in range(2):
                                kt = 2 * j + kk
                                o = S * kk + n * P
                                mm = three(bank[b + n][:, :], (wh[:, s, o:o + P], wl[:, s, o:o + P]),
                                           (src[0][:, kt, :], src[1][:, kt, :]),
                                           j == 0 and kk == 0, last and kk == 1)
                            mm.then_inc(pieces, 1)
            for i in range(2):
                for n in range(NT):
                    held[banks_of(G_PLE - 2 + i) + n] = NT * (G_PLE - 2 + i) + n

            for n in range(2):
                pe.wait_ge(tile_read, NT * (G_PLE - 1) + n + 1)
            pe.wait_ge(ss_ready, 3 * KT)
            stat(4, ssq)
            pe.wait_ge(p_copied, 2)
            for i in range(4):
                if i == 3:
                    pe.wait_ge(ss_ready, 4 * KT)
                    stat(5, ssq2)
                unit(U_PLE + i, G_PLE + i, X, (KT - 2, KT - 1), None, True, True, inc=5 if i == 0 else 1)

            need = (xl_ready, XL_GATE)
            pe.wait_ge(ffrow, 3)
            group(U_GATE, G_GATE, need)
            pe.wait_ge(tile_read, NT * G_GATE)
            pe.wait_ge(ss_ready, 5 * KT)
            stat(3, ssq)
            pe.wait_ge(row_ready, 3)
            for i in range(3):
                group(U_GATE + 8 * (i + 1), G_GATE + 1 + i)
            pe.wait_ge(tile_read, NT * (G_GATE + 3))
            pe.wait_ge(ss_ready, 6 * KT)
            stat(4, ssq2)

        @block.scalar
        def _(act):
            link = linker(act, act_chain)

            def split(u):
                act.wait_ge(raw_in[u % DEPTH], 16 * (u // DEPTH + 1))
                if u >= DEPTH:
                    act.wait_ge(pieces, 4 * (u - DEPTH + 1))
                act.activation(wh[:, u % DEPTH, :], raw[:, u % DEPTH, :], ACT.Copy).then_inc(hi_ready, 1)

            def done(u, n):
                act.wait_ge(pieces, 4 * u + n + 1)

            sq = [0]

            def square(src, bar=None):
                i = sq[0]
                if i >= 2:
                    act.wait_ge(ss_ready, i - 1)
                act.activation(tmp[:, i % 2, :], src, ACT.Square).then_inc(sq_ready, 1)
                sq[0] += 1

            def inverse_rms(dst, src, n=1.0 / D):
                link(act.activation(dst, src, ACT.Ln, scale=n, bias=eps[:, :]))
                return act.activation(dst, dst, ACT.Exp, scale=-0.5)

            act.wait_ge(par_in, 16)
            for j in range(8):
                act.wait_ge(x_in[j], 16)
                for kt in (2 * j, 2 * j + 1):
                    act.activation(xh[:, kt, :], hb[:, kt, :], ACT.Copy,
                                   scale=g(C_MIX_PRE, kt)).then_inc(xh_ready, 1)
                split(j)
                for kt in (2 * j, 2 * j + 1):
                    square(hb[:, kt, :])

            def stat_x():
                act.wait_ge(consts, 4)
                act.wait_ge(stat_mm, 1)
                link(inverse_rms(row[:, :], bank[4][:, :]))
                inverse_rms(tokf[:, :], bank[5][:, 0:2 * TT:2]).then_inc(row_ready, 1)

            def v_high(u):
                act.wait_ge(row_ready, 1)
                if u > U_V0 + 7:
                    act.wait_ge(n_mm, HH)
                for t in range(TT):
                    done(u, t)
                    act.activation(vh[:, t, :, 0:P], bank[t][:, :].rearrange("p (h d) -> p h d", h=HH),
                                   ACT.Copy, scale=tokf[:, t:t + 1]).then_inc(vh_ready, 1)

            def forget_ln():
                act.wait_ge(g_x, 1)
                link(act.activation(dw[0:H, 0:S], tmp[0:H, 1, :], ACT.Abs))
                link(act.activation(dw[0:H, 0:S], dw[0:H, 0:S], ACT.Exp, scale=-1.0))
                act.activation(dw[0:H, 0:S], dw[0:H, 0:S], ACT.Ln, bias=1.0).then_inc(g_ln, 1)

            def floor_exp():
                act.wait_ge(c_ready, 1)
                act.activation(colt[:, BLOCKS:, :], colt[:, BLOCKS:, :], ACT.Exp).then_inc(em_ready, 1)

            def sigmoid_o(b):
                for n in range(NT):
                    act.wait_ge(tile_read, NT * (G_O1 if b else G_O0) + n + 1)
                    act.activation(hb[:, HH * b + n, :], hb[:, HH * b + n, :], ACT.Sigmoid).then_inc(sig_ready, 1)

            def silu(i):
                dst = (qh, kh)[(i // NT) % 2]
                act.wait_ge(y_ready, i + 1)
                if i >= 2:
                    act.wait_ge(qk_l, i - 1)
                act.activation(tmp[:, i % 2, :], dw[:, S * (i % 2):S * (i % 2) + S], ACT.Silu).then_inc(qk_f, 1)
                act.wait_ge(qk_f, i + 1)
                act.activation(dst[:, i % NT, :], tmp[:, i % 2, :], ACT.Copy).then_inc(qk_h, 1)

            def exps(h):
                act.wait_ge(diag_ready, h + 1)
                for j in range(TT):
                    act.activation(dw[:, j * P:(j + 1) * P], dw[:, j * P:(j + 1) * P], ACT.Exp,
                                   bias=colt[:, j, h:h + 1])
                for i, (j, t) in enumerate(OFF):
                    o = (TT + i) * P
                    e = act.activation(dw[:, o:o + P], bank[4][:, t * P:(t + 1) * P], ACT.Exp,
                                       bias=colt[:, TT + i, h:h + 1])
                e.then_inc(d_ready, 1)

            def p_high(h):
                for i, (a, b) in enumerate(P_PARTS):
                    act.wait_ge(p_f, 3 * h + i + 1)
                    if h:
                        act.wait_ge(n_mm, h)
                    act.activation(ph[:, a:b], dw[:, a:b], ACT.Copy).then_inc(p_h, 1)

            def cell_scale(h):
                act.wait_ge(cs_ready, h + 1)
                inverse_rms(crs[:, :], cssq[:, :], 1.0 / P).then_inc(cr_ready, 1)

            def pool_high(i):
                dst = (qh, kh)[i // NT]
                act.wait_ge(pool_f, i + 1)
                act.activation(dst[:, i % NT, :], tmp[:, i % 2, :], ACT.Copy).then_inc(pool_h, 1)

            def cell_high(kt):
                act.wait_ge(cell_ready, kt + 1)
                act.activation(xh[:, kt, :], hb[:, kt, :], ACT.Copy).then_inc(xh_ready, 1)

            def pooled_high(b, u):
                for n in range(NT):
                    done(u, n)
                    act.activation(xh[:, 8 + NT * b + n, :], bank[4 + n][:, :], ACT.Copy,
                                   scale=g(C_POOL, NT * b + n)).then_inc(xh_ready, 1)

            def mix_squares(i):
                for n in range(NT):
                    act.wait_ge(tile_read, NT * (G_OUT + i) + n + 1)
                    square(acc[:, NT * i + n, :])

            def post_high(stage, kt, col):
                act.wait_ge(h_ready, KT * (stage - 2) + kt + 1)
                act.activation(xh[:, kt, :], hb[:, kt, :], ACT.Copy, scale=g(col, kt)).then_inc(xh_ready, 1)

            def row_stat(n_stat, dst, b):
                act.wait_ge(stat_mm, n_stat)
                return inverse_rms(dst, bank[b][:, :])

            during = {u: [] for u in range(UNITS)}
            before = {u: [] for u in range(UNITS)}

            def at(u, f, *args, first=False):
                (before if first else during)[u].append(lambda: f(*args))

            at(U_V0 + 6, stat_x)
            at(U_V0 + 7, v_high, U_V0 + 7)
            at(U_O0 + 2, forget_ln)
            at(U_O0 + 6, floor_exp)
            at(U_Q0, sigmoid_o, 0)
            for b, (uk, uo) in enumerate(((U_K0, U_O1), (U_K1, U_U0))):
                for n in range(NT):
                    at(uk + n, silu, 8 * b + n)
                for n in range(NT):
                    at(uo + n * 3 // 4, silu, 8 * b + NT + n)
                h0 = HH * b
                at(uo + 3, exps, h0)
                for i in range(HH):
                    at(uo + 4 + 2 * i, p_high, h0 + i)
                    if i + 1 < HH:
                        at(uo + 4 + 2 * i, exps, h0 + i + 1)
                    at(uo + 5 + 2 * i, cell_scale, h0 + i)
            at(U_O1 + 12, sigmoid_o, 1)
            at(U_V1 + 7, v_high, U_V1 + 7)
            for n in range(NT):
                at(U_U1 + 5 + n // 2, pool_high, n)
            for kt in range(H):
                at(U_POOL0, cell_high, kt, first=True)
            before[U_POOL0].insert(0, lambda: act.wait_ge(pieces, 4 * U_POOL0))
            at(U_POOL0, pooled_high, 0, U_POOL0)
            for n in range(NT):
                at(U_OUT0A + 1 + n // 2, pool_high, NT + n)
            at(U_POOL1, pooled_high, 1, U_POOL1)
            for i in range(3):
                at(U_OUT0B + 8 * i + 4, mix_squares, i)
            at(U_OUT1 + 23, mix_squares, 3)

            for u in range(5, U_FF):
                for f in before[u]:
                    f()
                split(u + LEAD)
                for f in during[u]:
                    f()

            row_stat(2, row[:, :], 3).then_inc(row_ready, 1)

            def hidden(c, j):
                t = HT * c + j
                act.wait_ge(tile_read, 6 * NT * c + (NT * G_FF + j + 1))
                r = tmp[:, j % 2, :]
                act.activation(r, r, ACT.Square).then_inc(ff_sq, 1)
                act.wait_ge(ff_sq, t + 1)
                act.activation(hidh[:, j, :], r, ACT.Copy).then_inc(hid_h, 1)

            for l in range(FF_UNITS):
                if l < 8:
                    post_high(2, 2 * l, C_FF_PRE)
                    post_high(2, 2 * l + 1, C_FF_PRE)
                split(U_FF + l + LEAD)
                if l == 8:
                    for kt in range(KT):
                        square(hb[:, kt, :])
                if l in (8, 16):
                    for n in range(NT):
                        j = NT * (l // 8 - 1) + n
                        hidden(0, j)
            with act.Fori(1, CHUNKS) as c:
                for l in range(FF_UNITS):
                    u = U_FF + l + LEAD
                    act.wait_ge(raw_in[u % DEPTH], 16 * FF_UNITS // DEPTH * c + 16 * (u // DEPTH + 1))
                    act.wait_ge(pieces, 4 * FF_UNITS * c + 4 * (u - DEPTH + 1))
                    act.activation(wh[:, u % DEPTH, :], raw[:, u % DEPTH, :], ACT.Copy).then_inc(hi_ready, 1)
                    if l in (8, 16):
                        for n in range(NT):
                            j = NT * (l // 8 - 1) + n
                            hidden(c, j)

            act.wait_ge(stat_mm, 3)
            act.activation(row[:, :], bank[4][:, :], ACT.Ln, scale=1.0 / D, bias=eps[:, :]).then_inc(ffrow, 1)
            split(U_P + LEAD)
            act.wait_ge(tile_read, NT * G_PLE)
            for u in range(U_PLE, U_GATE):
                if u < U_PLE + 2:
                    for m in range(8 * (u - U_PLE), 8 * (u - U_PLE) + 8):
                        square(acc[:, m, :])
                split(u + LEAD)
                if u == U_PLE + 3:
                    act.wait_ge(ss_ready, 4 * KT)
                    act.activation(tmp[:, 0, :], row[:, :], ACT.Exp, scale=-2.0).then_inc(ffrow, 1)
                    act.wait_ge(ffrow_v, 1)
                    link(act.activation(tmp[:, 1, :], tmp[:, 0, :], ACT.Ln, bias=eps[:, :]))
                    act.activation(tmp[:, 0, :], tmp[:, 1, :], ACT.Copy, scale=0.5).then_inc(ffrow, 1)
                    act.wait_ge(ffrow_v, 2)
                    act.activation(row[:, :], tmp[:, 0, :], ACT.Exp, scale=-1.0).then_inc(ffrow, 1)

            def sigmoid_gate(i, n):
                m = NT * i + n
                act.wait_ge(tile_read, NT * (G_GATE + i) + n + 1)
                act.activation(acc[:, m, :], acc[:, m, :], ACT.Sigmoid).then_inc(gsig, 1)

            def final_square(m):
                act.wait_ge(prod_ready, m + 1)
                square(acc[:, m, :])
                act.activation(acc[:, m, :], acc[:, m, :], ACT.Copy, scale=g(C_PLE_POST, m)).then_inc(fin_g, 1)

            def gate_group(i):
                for n in range(NT):
                    sigmoid_gate(i, n)
                    if n:
                        final_square(NT * i + n - 1)
                final_square(NT * i + NT - 1)

            for u in range(U_GATE, UNITS):
                j = u - U_GATE
                if j < 8:
                    post_high(3, 2 * j, C_PLE_GATE)
                    post_high(3, 2 * j + 1, C_PLE_GATE)
                if u + LEAD < UNITS:
                    split(u + LEAD)
                if j == 8:
                    for kt in range(KT):
                        square(hb[:, kt, :])
                    row_stat(5, row[:, :], 3).then_inc(row_ready, 1)
                if j in (10, 17, 25):
                    gate_group((j - 9) // 8 if j != 10 else 0)
            gate_group(3)
            row_stat(6, row[:, :], 4).then_inc(row_ready, 1)
            ov = out_t.rearrange("(k p) t -> k p t", p=P)
            for i, m in enumerate(POOL_TILES):
                act.wait_ge(out_g, i + 1)
                act.dma_start(ov[m], hb[:, m, :]).then_inc(stored, 16)

        @block.vector
        def _(dve):
            link = linker(dve, dve_chain)

            def done(u, n):
                dve.wait_ge(pieces, 4 * u + n + 1)

            ss = [0]

            def add_square(dst):
                i = ss[0]
                dve.wait_ge(sq_ready, i + 1)
                if i % KT == 0:
                    dve.tensor_copy(dst[:, :], tmp[:, i % 2, :]).then_inc(ss_ready, 1)
                else:
                    dve.wait_ge(ss_ready, i)
                    dve.tensor_tensor(dst[:, :], dst[:, :], tmp[:, i % 2, :], ALU.add).then_inc(ss_ready, 1)
                ss[0] += 1

            link(*[dve.memset(vh[:, t, :, P:P + 1].bitcast(F32), 1.0) for t in range(TT)],
                 *[dve.memset(vh[:, t, :, P + 1:P + 2].bitcast(F32), 0.0) for t in range(TT)],
                 *[dve.memset(vl[:, t, :, P:P + 2].bitcast(F32), 0.0) for t in range(TT)],
                 *[dve.memset(win[:, t:t + 1], 1.0 / (t + 1)) for t in range(16)])

            dve.wait_ge(par_in, 16)
            for j in range(8):
                dve.wait_ge(x_in[j], 16)
                for kt in (2 * j, 2 * j + 1):
                    dve.wait_ge(xh_ready, kt + 1)
                    dve.scalar_tensor_tensor(out=xl[:, kt, :], in0=hb[:, kt, :], scalar=g(C_MIX_PRE, kt),
                                             in1=xh[:, kt, :].bitcast(F32), op0=ALU.mult,
                                             op1=ALU.subtract).then_inc(xl_ready, 1)
                for kt in (2 * j, 2 * j + 1):
                    add_square(ssq)

            def v_low(b, u):
                for t in range(TT):
                    dve.wait_ge(vh_ready, NT * b + t + 1)
                    shape = bank[t][:, :].rearrange("p (h d) -> p h d", h=HH)
                    dve.scalar_tensor_tensor(out=vl[:, t, :, 0:P], in0=shape, scalar=tokf[:, t:t + 1],
                                             in1=vh[:, t, :, 0:P].bitcast(F32), op0=ALU.mult,
                                             op1=ALU.subtract).then_inc(tile_read, 1)

            def scaled(u, at_tile):
                for n in range(NT):
                    done(u, n)
                    dve.tensor_tensor(hb[:, at_tile + n, :], bank[n][:, :], row[:, :],
                                      ALU.mult).then_inc(tile_read, 1)

            v_low(0, U_V0 + 7)

            dve.wait_ge(g_mm, 1)
            for t in range(TT):
                e = dve.tensor_scalar(gsb[:, t, :], bank[6][:, 2 * H * t:2 * H * (t + 1)],
                                      tokf[:, t:t + 1], None, ALU.mult)
            e.then_inc(g_sb, 1)
            dve.wait_ge(g_tr, 1)
            gi, fg = tmp[0:H, 0, :], tmp[0:H, 1, :]
            dve.tensor_scalar(fg, bank[5][0:H, :], par[0:H, C_BIAS + 1:C_BIAS + 2], None,
                              ALU.add).then_inc(g_x, 1)
            link(dve.tensor_scalar(gi, bank[7][0:H, :], par[0:H, C_BIAS:C_BIAS + 1], None, ALU.add))
            dve.wait_ge(g_ln, 1)
            link(dve.scalar_tensor_tensor(out=fg, in0=fg, scalar=0.0, in1=dw[0:H, 0:S],
                                          op0=ALU.min, op1=ALU.subtract))
            bb = dw[0:H, S:2 * S]
            for t in range(TT):
                o = slice(t * P, (t + 1) * P)
                e = dve.tensor_tensor_scan(bb[:, o], ones[0:H, :], fg[:, o], 0.0, ALU.mult, ALU.add)
                link(e)
            link(dve.tensor_tensor(gi, gi, bb, ALU.subtract))
            for t in range(TT):
                o = slice(t * P, (t + 1) * P)
                link(dve.tensor_tensor_scan(ml[:, o], gi[:, o], gi[:, o], mp[:, t:t + 1] if t else 0.0,
                                            ALU.max, ALU.max))
                if t + 1 < TT:
                    e = (t + 1) * P
                    link(dve.tensor_tensor(mp[:, t + 1:t + 2], ml[:, e - 1:e], bb[:, e - 1:e], ALU.add))
            link(dve.tensor_tensor(fg, bb, ml, ALU.add))
            link(dve.tensor_scalar(fg, fg, -1.0, EXP_MAX, ALU.mult, ALU.min))
            for i, (j, t) in enumerate(OFF):
                o, e = pair_at(i), t * P
                src = gi[:, j * P:(j + 1) * P] if t == j + 1 else dw[0:H, pair_at(i - 1):pair_at(i - 1) + P]
                ins = dve.tensor_scalar(dw[0:H, o:o + P], src, bb[:, e - 1:e], None, ALU.add)
                if i + 1 < len(OFF):
                    link(ins)
            ins.then_inc(c_sb, 1)
            dve.wait_ge(c_tr, 1)
            dve.tensor_copy(colt[:, :, :], bank[6][:, 0:H * (BLOCKS + TT)].rearrange(
                "p (i h) -> p i h", h=H)).then_inc(c_ready, 1)

            scaled(U_O0 + 7, 0)

            def conv(i, tile, wtile):
                y = dw[:, S * (i % 2):S * (i % 2) + S]
                x = hb[:, tile, :]

                def w(k):
                    return par[:, C_CONV + CONV * wtile + k:C_CONV + CONV * wtile + k + 1]
                link(dve.tensor_scalar(y, x, w(CONV - 1), None, ALU.mult))
                for s in range(1, CONV):
                    ins = dve.scalar_tensor_tensor(out=y[:, s:], in0=x[:, :S - s], scalar=w(CONV - 1 - s),
                                                   in1=y[:, s:], op0=ALU.mult, op1=ALU.add)
                    if s < CONV - 1:
                        link(ins)
                ins.then_inc(y_ready, 1)

            def qk_low(i):
                dst, hi = ((ql, qh), (kl, kh))[(i // NT) % 2]
                dve.wait_ge(qk_h, i + 1)
                dve.tensor_tensor(dst[:, i % NT, :], tmp[:, i % 2, :], hi[:, i % NT, :].bitcast(F32),
                                  ALU.subtract).then_inc(qk_l, 1)

            def qk(b, is_k, u, g_):
                base = 8 + NT * is_k
                scaled(u + 7, base)
                dve.wait_ge(tile_read, NT * (g_ + 1))
                i0 = 8 * b + NT * is_k
                for n in range(NT):
                    conv(i0 + n, base + n, 8 * is_k + NT * b + n)
                    if n:
                        qk_low(i0 + n - 1)
                qk_low(i0 + NT - 1)

            def select(h):
                dve.tensor_scalar(nsel[:, h % 2, :], ones[0:H, :], ident[0:H, h:h + 1], -1.0,
                                  ALU.mult, ALU.mult).then_inc(sel_ready, 1)

            def diag(h):
                dve.wait_ge(r_mm, h + 1)
                if h % HH:
                    dve.wait_ge(p_l, 3 * h)
                dve.tensor_tensor(dw[:, 0:S].rearrange("p (t n) -> p t n", t=TT),
                                  bank[4][:, :].rearrange("p (t n) -> p t n", t=TT),
                                  mask[:, :].unsqueeze(1).to_broadcast([P, TT, P]),
                                  ALU.add).then_inc(diag_ready, 1)

            def weigh(h):
                dve.wait_ge(d_ready, h + 1)
                for i, (a, b) in enumerate(P_PARTS):
                    dve.wait_ge(s_mm, 3 * h + i + 1)
                    dve.scalar_tensor_tensor(out=dw[:, a:b], in0=bank[5 + i][:, 0:b - a], scalar=P ** -0.5,
                                             in1=dw[:, a:b], op0=ALU.mult, op1=ALU.mult).then_inc(p_f, 1)
                for i, (a, b) in enumerate(P_PARTS):
                    dve.wait_ge(p_h, 3 * h + i + 1)
                    dve.tensor_tensor(pl[:, a:b], dw[:, a:b], ph[:, a:b].bitcast(F32),
                                      ALU.subtract).then_inc(p_l, 1)

            def normalise(h):
                dve.wait_ge(n_mm, h + 1)
                dve.wait_ge(em_ready, 1)
                link(dve.tensor_copy(den[:, 0:3],
                                     bank[5][:, 0:390].rearrange("p (t n) -> p t n", n=130)[:, :, P]),
                     dve.tensor_copy(den[:, 3:4], bank[6][:, P:P + 1]))
                link(dve.scalar_tensor_tensor(out=den[:, :], in0=den[:, :], scalar=-1.0, in1=den[:, :],
                                              op0=ALU.mult, op1=ALU.max))
                link(dve.tensor_tensor(den[:, :], den[:, :], colt[:, BLOCKS:, h], ALU.max))
                link(dve.reciprocal(den[:, :], den[:, :]))
                for t in range(TT):
                    src = bank[5][:, 130 * t:130 * t + P] if t < 3 else bank[6][:, 0:P]
                    e = dve.tensor_scalar(cn[:, t * P:(t + 1) * P], src, den[:, t:t + 1], None, ALU.mult)
                e.then_inc(n_read, 1)
                dve.wait_ge(n_read, h + 1)
                for t in range(TT):
                    c = cn[:, t * P:(t + 1) * P]
                    e = dve.tensor_tensor_reduce(out=tmp[:, 1, t * P:(t + 1) * P], in0=c, in1=c, scale=1.0,
                                                 scalar=0.0, op0=ALU.mult, op1=ALU.add,
                                                 accum_out=cssq[:, t:t + 1])
                e.then_inc(cs_ready, 1)

            def scale_cell(h):
                dve.wait_ge(cr_ready, h + 1)
                for t in range(TT):
                    c = cn[:, t * P:(t + 1) * P]
                    e = dve.tensor_scalar(c, c, crs[:, t:t + 1], None, ALU.mult)
                e.then_inc(cn_ready, 1)

            def gate_cell(h):
                dve.wait_ge(tr_mm, h + 1)
                dve.wait_ge(sig_ready, h + 1)
                dve.scalar_tensor_tensor(out=hb[:, h, :], in0=bank[7][:, :], scalar=g(C_MLSTM, h),
                                         in1=hb[:, h, :], op0=ALU.mult, op1=ALU.mult).then_inc(cell_ready, 1)

            def half(h0, middle):
                select(h0)
                select(h0 + 1)
                diag(h0)
                for i in range(HH):
                    h = h0 + i
                    if i == 2:
                        middle()
                    if i:
                        scale_cell(h - 1)
                    weigh(h)
                    if i + 1 < HH:
                        diag(h + 1)
                        if i + 2 < HH:
                            select(h + 2)
                    if i:
                        gate_cell(h - 1)
                    normalise(h)
                scale_cell(h0 + HH - 1)
                gate_cell(h0 + HH - 1)

            qk(0, 0, U_Q0, G_Q0)
            qk(0, 1, U_K0, G_K0)
            half(0, lambda: scaled(U_O1 + 7, HH))
            v_low(1, U_V1 + 7)
            qk(1, 0, U_Q1, G_Q1)
            qk(1, 1, U_K1, G_K1)
            half(HH, lambda: scaled(U_U0 + 7, 8))

            def pooling(i):
                w = WINDOWS[i // 2]
                u = hb[:, 8 + i, :]
                src, d, flip = u, 1, 0
                if i:
                    dve.wait_ge(pool_f, i)
                while d < w:
                    dst = dw[:, S * flip:S * flip + S]
                    link(dve.tensor_copy(dst[:, 0:d], src[:, 0:d]),
                         dve.tensor_tensor(dst[:, d:], src[:, d:], src[:, :S - d], ALU.add))
                    src, d, flip = dst, 2 * d, 1 - flip
                out = tmp[:, i % 2, :]
                link(dve.tensor_tensor(out[:, 0:w - 1], src[:, 0:w - 1], win[:, 0:w - 1], ALU.mult))
                link(dve.tensor_tensor(out[:, 0:w - 1], out[:, 0:w - 1], u[:, 0:w - 1], ALU.subtract))
                dve.scalar_tensor_tensor(out=out[:, w - 1:], in0=src[:, w - 1:], scalar=1.0 / w,
                                         in1=u[:, w - 1:], op0=ALU.mult, op1=ALU.subtract).then_inc(pool_f, 1)

            def pool_low(i):
                dst, hi = ((ql, qh), (kl, kh))[i // NT]
                dve.wait_ge(pool_h, i + 1)
                dve.tensor_tensor(dst[:, i % NT, :], tmp[:, i % 2, :], hi[:, i % NT, :].bitcast(F32),
                                  ALU.subtract).then_inc(pool_l, 1)

            def pool_half(b):
                for n in range(NT):
                    pooling(NT * b + n)
                    if n:
                        pool_low(NT * b + n - 1)
                pool_low(NT * b + NT - 1)

            dve.wait_ge(tile_read, NT * (G_U0 + 1))
            pool_half(0)
            scaled(U_U1 + 7, 12)
            dve.wait_ge(cell_ready, H)
            for kt in range(H):
                dve.wait_ge(xh_ready, KT + kt + 1)
                dve.tensor_tensor(xl[:, kt, :], hb[:, kt, :], xh[:, kt, :].bitcast(F32),
                                  ALU.subtract).then_inc(xl_ready, 1)

            def pooled_low(b):
                for n in range(NT):
                    kt = 8 + NT * b + n
                    dve.wait_ge(xh_ready, KT + kt + 1)
                    dve.scalar_tensor_tensor(out=xl[:, kt, :], in0=bank[4 + n][:, :],
                                             scalar=g(C_POOL, NT * b + n), in1=xh[:, kt, :].bitcast(F32),
                                             op0=ALU.mult, op1=ALU.subtract).then_inc(tile_read, 1)

            pooled_low(0)
            dve.wait_ge(tile_read, NT * (G_POOL0 + 1))
            pool_half(1)
            pooled_low(1)

            for i in range(NT):
                u = U_OUT0B + 3 + 8 * i
                for n in range(NT):
                    done(u, n)
                    dve.tensor_copy(acc[:, NT * i + n, :], bank[banks_of(G_OUT + i) + n][:, :])\
                       .then_inc(tile_read, 1)
                    if n:
                        add_square(ssq)
                add_square(ssq)

            def post_norm(stage, post, pre):
                def low(kt):
                    dve.wait_ge(xh_ready, KT * stage + kt + 1)
                    dve.scalar_tensor_tensor(out=xl[:, kt, :], in0=hb[:, kt, :], scalar=g(pre, kt),
                                             in1=xh[:, kt, :].bitcast(F32), op0=ALU.mult,
                                             op1=ALU.subtract).then_inc(xl_ready, 1)
                for kt in range(KT):
                    link(dve.tensor_tensor(acc[:, kt, :], acc[:, kt, :], row[:, :], ALU.mult))
                    dve.scalar_tensor_tensor(out=hb[:, kt, :], in0=acc[:, kt, :], scalar=g(post, kt),
                                             in1=hb[:, kt, :], op0=ALU.mult, op1=ALU.add).then_inc(h_ready, 1)
                    if kt:
                        low(kt - 1)
                low(KT - 1)

            dve.wait_ge(row_ready, 2)
            dve.wait_ge(xr_in, 16 * KT // 2)
            dve.wait_ge(tile_read, NT * G_FF)
            post_norm(2, C_MIX_POST, C_FF_PRE)
            for kt in range(KT):
                add_square(ssq)
            link(dve.memset(acc[:, :, :], 0.0))

            with dve.Fori(0, CHUNKS) as c:
                def low(j):
                    dve.wait_ge(hid_h, HT * c + (j + 1))
                    dve.tensor_tensor(hidl[:, j, :], tmp[:, j % 2, :], hidh[:, j, :].bitcast(F32),
                                      ALU.subtract).then_inc(hid_l, 1)
                for k in range(2 + NT):
                    u = U_FF + (8 * k + 7 if k < 2 else 16 + 4 * (k - 2) + 3)
                    for n in range(NT):
                        b = bank[banks_of(G_FF + k) + n]
                        dve.wait_ge(pieces, 4 * FF_UNITS * c + (4 * u + n + 1))
                        if k < 2:
                            j = NT * k + n
                            if j >= 2:
                                dve.wait_ge(hid_l, HT * c + (j - 1))
                            dve.tensor_scalar(tmp[:, j % 2, :], b[:, :], 0.0, None, ALU.max)\
                               .then_inc(tile_read, 1)
                            if j:
                                low(j - 1)
                            if j == HT - 1:
                                low(j)
                        else:
                            m = NT * (k - 2) + n
                            dve.tensor_tensor(acc[:, m, :], b[:, :], acc[:, m, :], ALU.add)\
                               .then_inc(tile_read, 1)

            dve.wait_ge(lo_ready, U_P + 1)
            s = U_P % DEPTH
            dve.tensor_copy(xh[:, KT - 2:, :], wh[:, s, :].bitcast(F32).rearrange("p (k t) -> p k t", k=2))\
               .then_inc(p_copied, 1)
            dve.tensor_copy(xl[:, KT - 2:, :], wl[:, s, :].bitcast(F32).rearrange("p (k t) -> p k t", k=2))\
               .then_inc(p_copied, 1)

            def embedding(i):
                for n in range(NT):
                    done(U_PLE + i, n)
                    dve.tensor_copy(emb[:, NT * i + n, :], bank[n][:, :]).then_inc(tile_read, 1)

            for m in range(KT):
                add_square(ssq2)
                if m in (6, 12):
                    embedding(m // 6 - 1)
            embedding(2)
            dve.wait_ge(ffrow, 2)
            dve.wait_ge(stat_mm, 4)
            dve.scalar_tensor_tensor(out=tmp[:, 0, :], in0=bank[5][:, :], scalar=1.0 / D, in1=tmp[:, 0, :],
                                     op0=ALU.mult, op1=ALU.mult).then_inc(ffrow_v, 1)
            dve.wait_ge(ffrow, 3)
            dve.tensor_tensor(tmp[:, 0, :], tmp[:, 0, :], row[:, :], ALU.add).then_inc(ffrow_v, 1)
            embedding(3)
            dve.wait_ge(ffrow, 4)
            post_norm(3, C_FF_POST, C_PLE_GATE)
            for kt in range(KT):
                add_square(ssq)

            dve.wait_ge(row_ready, 3)
            for i in range(NT):
                def product(m):
                    dve.wait_ge(gsig, m + 1)
                    dve.tensor_tensor(acc[:, m, :], acc[:, m, :], emb[:, m, :], ALU.mult)\
                       .then_inc(prod_ready, 1)
                for n in range(NT + 2):
                    m = NT * i + n
                    if n < NT:
                        done(U_GATE + 8 * i + 7, n)
                        dve.tensor_tensor(acc[:, m, :], bank[banks_of(G_GATE + i) + n][:, :], row[:, :],
                                          ALU.mult).then_inc(tile_read, 1)
                    if 1 <= n <= NT:
                        product(m - 1)
                    if n >= 2:
                        add_square(ssq2)
            dve.wait_ge(row_ready, 4)
            for m in VECTOR_TILES:
                dve.wait_ge(fin_g, m + 1)
                link(dve.tensor_tensor(acc[:, m, :], acc[:, m, :], row[:, :], ALU.mult))
                dve.tensor_tensor(hb[:, m, :], hb[:, m, :], acc[:, m, :], ALU.add).then_inc(out_v, 1)


def pair_at(i):
    return i * P if i < 4 else 2 * S + (i - 4) * P


P_PARTS = [(0, S), (S, S + 3 * P), (S + 3 * P, S + 6 * P)]
VECTOR_TILES = [m for m in range(KT) if m % 3 != 1]
POOL_TILES = [m for m in range(KT) if m % 3 == 1]


def pack(w):
    k, n = w.shape
    return w.reshape(k // 256, 2, P, n // 512, 512).transpose(3, 0, 2, 1, 4).reshape(
        n // 512, k // 256, P, 1024)


def kernel(x, p, w_in, b_gates, w_qk_conv, g_mlstm, w_pool, pool_scale, w_out, g_mix_pre, g_mix_post,
           w_ff1, w_ff2, g_ff_pre, g_ff_post, w_ple_proj, w_ple_gate, g_ple_gate, g_ple_post):
    import numpy as np
    import concourse.bacc as bacc
    from concourse.bass_utils import run_bass_kernel_spmd

    a = {k: np.asarray(v)[0] for k, v in dict(
        x=x, p=np.asarray(p)[0], w_in=w_in, b_gates=b_gates, conv=w_qk_conv, g_mlstm=g_mlstm,
        w_pool=w_pool, pool_scale=pool_scale, w_out=w_out, g_mix_pre=g_mix_pre, g_mix_post=g_mix_post,
        w_ff1=w_ff1, w_ff2=w_ff2, g_ff_pre=g_ff_pre, g_ff_post=g_ff_post, w_ple_proj=w_ple_proj,
        w_ple_gate=w_ple_gate, g_ple_gate=g_ple_gate, g_ple_post=g_ple_post).items()}
    w = a["w_in"]
    m = D // 2
    q, k, v, o = (pack(w[:, i * m:(i + 1) * m]) for i in range(4))
    gates = w[:, 4 * m:4 * m + 2 * H]
    u = pack(w[:, 4 * m + 2 * H:])
    gates_u = np.zeros((1, P, 1024), np.float32)
    gates_u[0, :, 0:KT * 2 * H] = gates.reshape(KT, P, 2 * H).transpose(1, 0, 2).reshape(P, -1)
    pools = a["w_pool"].reshape(2, 2, 2, P, 256).transpose(0, 3, 1, 2, 4).reshape(2, P, 1024)
    wo = pack(a["w_out"])
    ff1 = pack(a["w_ff1"]).reshape(CHUNKS, 16, P, 1024)
    ff2 = pack(a["w_ff2"]).reshape(4, CHUNKS, 4, P, 1024).transpose(1, 0, 2, 3, 4).reshape(
        CHUNKS, 16, P, 1024)
    ff = np.concatenate([ff1, ff2], axis=1).reshape(-1, P, 1024)
    p_unit = a["p"].T.reshape(2, P, S).transpose(1, 0, 2).reshape(1, P, 1024)
    stream = np.concatenate([
        v[0], gates_u, o[0], q[0], k[0], o[1], v[1], q[1], k[1], u[0], u[1], pools[0:1], wo[0, 0:4],
        pools[1:2], wo[0, 4:8], wo[1], wo[2], wo[3], ff, p_unit,
        pack(a["w_ple_proj"]).reshape(4, P, 1024), pack(a["w_ple_gate"]).reshape(32, P, 1024)])
    assert stream.shape[0] == UNITS
    par = np.zeros((P, PARAMS), np.float32)
    for c, name in ((C_MIX_PRE, "g_mix_pre"), (C_MIX_POST, "g_mix_post"), (C_FF_PRE, "g_ff_pre"),
                    (C_FF_POST, "g_ff_post"), (C_PLE_GATE, "g_ple_gate"), (C_PLE_POST, "g_ple_post"),
                    (C_MLSTM, "g_mlstm"), (C_POOL, "pool_scale")):
        t = a[name].reshape(-1, P).T
        par[:, c:c + t.shape[1]] = t
    par[:, C_CONV:C_CONV + 16 * CONV] = a["conv"].reshape(CONV, 16, P).transpose(2, 1, 0).reshape(P, -1)
    par[0:H, C_BIAS:C_BIAS + 2] = a["b_gates"].reshape(2, H).T
    arrays = {"stream": np.ascontiguousarray(stream), "x_t": np.ascontiguousarray(a["x"].T), "params": par}

    nc = bacc.Bacc("TRN2", target_bir_lowering=False, num_devices=1, dynamic_dma_scratch_size=1024)
    aps = [nc.dram_tensor(n, arr.shape, F32, kind="ExternalInput").ap() for n, arr in arrays.items()]
    out = nc.dram_tensor("out_t", (D, S), F32, kind="ExternalOutput").ap()
    build(nc, *aps, out)
    r = run_bass_kernel_spmd(nc, [arrays], core_ids=[0])
    return np.ascontiguousarray(r.results[0]["out_t"].T)[None]
```

```python
from contextlib import ExitStack

import concourse.bass as bass
from concourse import mybir

F32 = mybir.dt.float32
F32R = mybir.dt.float32r
ALU = mybir.AluOpType
ACT = mybir.ActivationFunctionType

P = 128
S = 512
D = 2048
KT = D // P
H = 8
HH = H // 2
TT = S // P
NT = 4
CONV = 4
WINDOWS = (2, 4, 8, 16)
EPS = 1e-6
FF = 4 * D
CHUNKS = 8
HT = FF // CHUNKS // P
DEPTH = 4
LEAD = DEPTH - 1

U_V0 = 0
U_GATES = U_V0 + 8
U_O0 = U_GATES + 1
U_Q0 = U_O0 + 8
U_K0 = U_Q0 + 8
U_O1 = U_K0 + 8
U_V1 = U_O1 + 8
U_Q1 = U_V1 + 8
U_K1 = U_Q1 + 8
U_U0 = U_K1 + 8
U_U1 = U_U0 + 8
U_POOL0 = U_U1 + 8
U_OUT0A = U_POOL0 + 1
U_POOL1 = U_OUT0A + 4
U_OUT0B = U_POOL1 + 1
U_OUT1 = U_OUT0B + 4
U_FF = U_OUT1 + 24
FF_UNITS = 32
U_P = U_FF + CHUNKS * FF_UNITS
U_PLE = U_P + 1
U_GATE = U_PLE + 4
UNITS = U_GATE + 32

(G_V0, G_O0, G_Q0, G_K0, G_O1, G_V1, G_Q1, G_K1, G_U0, G_U1, G_POOL0, G_POOL1, G_OUT) = range(13)
G_FF = G_OUT + 4
G_PLE = G_FF + 6 * CHUNKS
G_GATE = G_PLE + 4

C_MIX_PRE, C_MIX_POST, C_FF_PRE, C_FF_POST, C_PLE_GATE, C_PLE_POST = (KT * i for i in range(6))
C_MLSTM = 6 * KT
C_POOL = C_MLSTM + H
C_CONV = C_POOL + 8
C_BIAS = C_CONV + 16 * CONV
PARAMS = C_BIAS + 2

OFF = [(0, 1), (0, 2), (0, 3), (1, 2), (1, 3), (2, 3)]
BLOCK = {(j, j): j for j in range(TT)} | {jt: TT + i for i, jt in enumerate(OFF)}
BLOCKS = len(BLOCK)
NEG = -1e30
XL_MIX = KT
XL_FF = XL_MIX + H
XL_GATE = XL_FF + KT
SQ_X, SQ_MIX, SQ_H, SQ_FF, SQ_G, SQ_END = ((0, 0), (16, 16), (32, 32), (47, 48), (63, 64), (78, 80))
EXP_MAX = 88.0


def banks_of(g):
    if g in (G_POOL0, G_POOL1):
        return 4
    if g < G_OUT:
        return 0
    if G_PLE <= g < G_GATE:
        return 4 if g == G_PLE + 2 else 0
    if g >= G_GATE:
        return 4 * ((g - G_GATE + 1) % 2)
    return 4 * ((g - G_OUT) % 2)


def build(nc, stream, x_t, params, out_t):
    ctx = ExitStack()
    with ctx:
        def sem(name):
            return ctx.enter_context(nc.semaphore(name))

        def sb(name, shape, dt=F32, stack=ctx):
            return stack.enter_context(nc.sbuf_tensor(name, shape, dt))

        hb = sb("hb", [P, KT, S])
        xh = sb("xh", [P, KT, S], F32R)
        xl = sb("xl", [P, KT, S], F32R)
        raw = sb("raw", [P, DEPTH, 1024])
        wh = sb("wh", [P, DEPTH, 1024], F32R)
        wl = sb("wl", [P, DEPTH, 1024], F32R)
        tmp = sb("tmp", [P, 2, S])
        row = sb("row", [P, S])
        ssq = sb("ssq", [P, S])
        ident = sb("ident", [P, P])
        ones = sb("ones", [P, P])
        mask = sb("mask", [P, P])
        par = sb("par", [P, PARAMS])
        eps = sb("eps", [P, 1])
        win = sb("win", [P, 16])
        tokf = sb("tokf", [P, TT])
        colt = sb("colt", [P, BLOCKS + TT, H])
        mp = sb("mp", [H, TT])
        nsel = sb("nsel", [H, 2, P])
        den = sb("den", [P, TT])
        cssq = sb("cssq", [P, TT])
        crs = sb("crs", [P, TT])
        mixer = ExitStack()
        with mixer:
            vh = sb("vh", [P, TT, HH, 130], F32R, mixer)
            vl = sb("vl", [P, TT, HH, 130], F32R, mixer)
            qh = sb("qh", [P, HH, S], F32R, mixer)
            ql = sb("ql", [P, HH, S], F32R, mixer)
            kh = sb("kh", [P, HH, S], F32R, mixer)
            kl = sb("kl", [P, HH, S], F32R, mixer)
            dw = sb("dw", [P, BLOCKS * P], F32, mixer)
            ph = sb("ph", [P, BLOCKS * P], F32R, mixer)
            pl = sb("pl", [P, BLOCKS * P], F32R, mixer)
        acc = sb("acc", [P, KT, S])
        hid_stack = ExitStack()
        with hid_stack:
            hidh = sb("hidh", [P, HT, S], F32R, hid_stack)
            hidl = sb("hidl", [P, HT, S], F32R, hid_stack)
        emb = sb("emb", [P, KT, S])
        ssq2 = sb("ssq2", [P, S])
        ml = ssq[0:H, :]
        cn = tmp[:, 0, :]

        bank = [ctx.enter_context(nc.psum_tensor(f"bank{i}", [P, 512], F32)) for i in range(8)]

        x_in = [sem(f"x_in{j}") for j in range(KT // 2)]
        par_in = sem("par_in")
        xr_in = sem("xr_in")
        raw_in = [sem(f"raw_in{s}") for s in range(DEPTH)]
        hi_ready = sem("hi_ready")
        lo_ready = sem("lo_ready")
        pieces = sem("pieces")
        tile_read = sem("tile_read")
        consts = sem("consts")
        xh_ready = sem("xh_ready")
        xl_ready = sem("xl_ready")
        sq_ready = sem("sq_ready")
        ss_ready = sem("ss_ready")
        stat_mm = sem("stat_mm")
        row_ready = sem("row_ready")
        vh_ready = sem("vh_ready")
        g_mm = sem("g_mm")
        g_sb = sem("g_sb")
        g_tr = sem("g_tr")
        g_ln = sem("g_ln")
        g_x = sem("g_x")
        c_sb = sem("c_sb")
        c_tr = sem("c_tr")
        c_ready = sem("c_ready")
        em_ready = sem("em_ready")
        sig_ready = sem("sig_ready")
        y_ready = sem("y_ready")
        qk_f = sem("qk_f")
        qk_h = sem("qk_h")
        qk_l = sem("qk_l")
        sel_ready = sem("sel_ready")
        r_mm = sem("r_mm")
        diag_ready = sem("diag_ready")
        d_ready = sem("d_ready")
        s_mm = sem("s_mm")
        p_f = sem("p_f")
        p_h = sem("p_h")
        p_l = sem("p_l")
        n_mm = sem("n_mm")
        n_read = sem("n_read")
        cs_ready = sem("cs_ready")
        cr_ready = sem("cr_ready")
        cn_ready = sem("cn_ready")
        tr_mm = sem("tr_mm")
        cell_ready = sem("cell_ready")
        pool_f = sem("pool_f")
        pool_h = sem("pool_h")
        pool_l = sem("pool_l")
        h_ready = sem("h_ready")
        scaled_acc = sem("scaled_acc")
        hid_h = sem("hid_h")
        hid_l = sem("hid_l")
        ff_sq = sem("ff_sq")
        p_copied = sem("p_copied")
        ffrow = sem("ffrow")
        ffrow_v = sem("ffrow_v")
        gsig = sem("gsig")
        prod_ready = sem("prod_ready")
        fin_g = sem("fin_g")
        dve_chain = sem("dve_chain")
        act_chain = sem("act_chain")
        pool_chain = sem("pool_chain")
        out_v = sem("out_v")
        out_g = sem("out_g")
        stored = sem("stored")

        block = ctx.enter_context(nc.Block())

        def linker(eng, chain):
            count = [0]

            def link(*instructions):
                for ins in instructions:
                    ins.then_inc(chain, 1)
                count[0] += len(instructions)
                eng.wait_ge(chain, count[0])
            return link

        def g(col, kt):
            return par[:, col + kt:col + kt + 1]

        @block.sync
        def _(sp):
            def load(u, first=False):
                sp.dma_start(raw[:, u % DEPTH, :], stream[u]).then_inc(raw_in[u % DEPTH], 16)

            xv = x_t.rearrange("(j k p) t -> j p k t", k=2, p=P)
            for j in range(KT // 2):
                sp.dma_start(hb[:, 2 * j:2 * j + 2, :], xv[j]).then_inc(x_in[j], 16)
                if j < DEPTH:
                    load(j)
                if j == 0:
                    sp.dma_start(par[:, :], params).then_inc(par_in, 16)

            def load_loop(lo, hi):
                with sp.Fori(lo, hi) as i:
                    for s in range(DEPTH):
                        sp.wait_ge(lo_ready, DEPTH * i + (s + 1 - DEPTH))
                        src = stream[bass.ds(DEPTH * i + s, 1)].rearrange("o p n -> p (o n)")
                        sp.dma_start(raw[:, s, :], src).then_inc(raw_in[s], 16)

            turn = (U_OUT1 + 12) // DEPTH
            load_loop(1, turn)
            sp.wait_ge(xl_ready, XL_MIX + H)
            sp.wait_ge(pool_l, 2 * NT)
            for j in range(KT // 2):
                sp.dma_start(hb[:, 2 * j:2 * j + 2, :], xv[j]).then_inc(xr_in, 16)
            load_loop(turn, UNITS // DEPTH)
            ov = out_t.rearrange("(k p) t -> k p t", p=P)
            for m in VECTOR_TILES:
                sp.wait_ge(out_v, VECTOR_TILES.index(m) + 1)
                sp.dma_start(ov[m], hb[:, m, :]).then_inc(stored, 16)
            sp.wait_ge(stored, 16 * KT)

        @block.gpsimd
        def _(pool):
            pool.memset(ones[:, :], 1.0).then_inc(consts, 1)
            pool.memset(eps[:, :], EPS).then_inc(consts, 1)
            pool.memset(ident[:, :], 1.0).then_inc(pool_chain, 1)
            pool.memset(mask[:, :], 0.0).then_inc(pool_chain, 1)
            pool.wait_ge(pool_chain, 2)
            pool.affine_select(out=ident[:, :], in_=ident[:, :], compare_op=ALU.is_equal, fill=0.0,
                               base=0, pattern=[[-1, P]], channel_multiplier=1).then_inc(consts, 1)
            pool.affine_select(out=mask[:, :], in_=mask[:, :], compare_op=ALU.is_ge, fill=NEG,
                               base=0, pattern=[[1, P]], channel_multiplier=-1).then_inc(consts, 1)

            def low(i, s):
                pool.wait_ge(hi_ready, DEPTH * i + (s + 1))
                pool.tensor_tensor(wl[:, s, :], raw[:, s, :], wh[:, s, :].bitcast(F32),
                                   ALU.subtract).then_inc(lo_ready, 1)

            def low_loop(lo, hi):
                with pool.Fori(lo, hi) as i:
                    for s in range(DEPTH):
                        low(i, s)

            def low_and_sum(lo, hi, first, base):
                for u in range(DEPTH * lo, DEPTH * hi):
                    low(u // DEPTH, u % DEPTH)
                    if 0 <= u - first < 8:
                        for kt in (2 * (u - first), 2 * (u - first) + 1):
                            if kt:
                                pool.wait_ge(sq_ready, base[0] + kt)
                                pool.wait_ge(ss_ready, base[1] + kt)
                                pool.tensor_tensor(ssq[:, :], ssq[:, :], tmp[:, kt % 2, :],
                                                   ALU.add).then_inc(ss_ready, 1)

            ff_lo, ff_hi = (U_FF + LEAD) // DEPTH, (U_FF + LEAD + 7) // DEPTH + 1
            g_lo, g_hi = (U_GATE + LEAD) // DEPTH, (U_GATE + LEAD + 7) // DEPTH + 1
            low_loop(0, ff_lo)
            low_and_sum(ff_lo, ff_hi, U_FF + LEAD, SQ_H)
            low_loop(ff_hi, g_lo)
            low_and_sum(g_lo, g_hi, U_GATE + LEAD, SQ_G)
            low_loop(g_hi, UNITS // DEPTH)
            pool.wait_ge(row_ready, 4)
            for i, m in enumerate(POOL_TILES):
                pool.wait_ge(fin_g, m + 1)
                pool.tensor_tensor(acc[:, m, :], acc[:, m, :], row[:, :], ALU.mult).then_inc(pool_chain, 1)
                pool.wait_ge(pool_chain, 3 + i)
                pool.tensor_tensor(hb[:, m, :], hb[:, m, :], acc[:, m, :], ALU.add).then_inc(out_g, 1)

        @block.tensor
        def _(pe):
            held = {}

            def claim(g_, n):
                b = banks_of(g_) + n
                if b in held:
                    pe.wait_ge(tile_read, held[b] + 1)
                held[b] = NT * g_ + n
                return bank[b]

            def three(out, a, b, first, last):
                pe.matmul(out, a[0], b[0], start=first, stop=False)
                pe.matmul(out, a[0], b[1], start=False, stop=False)
                return pe.matmul(out, a[1], b[0], start=False, stop=last)

            def weights(u, k, c0, c1):
                s = u % DEPTH
                return (wh[:, s, S * k + c0:S * k + c1], wl[:, s, S * k + c0:S * k + c1])

            def unit(u, g_, rhs, kts, need=None, first=True, last=True, tokens_out=False, inc=1,
                     busy=None):
                pe.wait_ge(lo_ready, u + 1)
                if need:
                    pe.wait_ge(need[0], need[1] + kts[1] + 1)
                for n in range(NT):
                    if busy and n == busy[0]:
                        pe.wait_ge(busy[1], 1)
                    out = claim(g_, n) if first else bank[banks_of(g_) + n]
                    for k, kt in enumerate(kts):
                        x = (rhs[0][:, kt, :], rhs[1][:, kt, :])
                        st, en = first and k == 0, last and k == 1
                        if tokens_out:
                            x = tuple(v[:, n * P:(n + 1) * P] for v in x)
                            mm = three(out[:, :], x, weights(u, k, 0, S), st, en)
                        else:
                            mm = three(out[:, :], weights(u, k, n * P, (n + 1) * P), x, st, en)
                    mm.then_inc(pieces, inc if n == 0 else 1)

            X = (xh, xl)

            def group(u0, g_, need=None, tokens_out=False, after=None):
                for j in range(KT // 2):
                    unit(u0 + j, g_, X, (2 * j, 2 * j + 1), need, j == 0, j == KT // 2 - 1, tokens_out)
                    if after and j in after:
                        after[j]()

            def stat(b, src, held_until=None):
                pe.matmul(bank[b][:, :], ones[:, :], src[:, :], start=True, stop=True).then_inc(stat_mm, 1)

            pe.wait_ge(consts, 4)
            for j in range(7):
                unit(U_V0 + j, G_V0, X, (2 * j, 2 * j + 1), (xl_ready, 0), j == 0, False, True)
            pe.wait_ge(ss_ready, KT)
            for t in range(TT):
                pe.matmul(bank[5][:, 2 * t:2 * t + 2], ssq[:, t * P:(t + 1) * P], ones[:, 0:2],
                          start=True, stop=True)
            stat(4, ssq)
            unit(U_V0 + 7, G_V0, X, (14, 15), (xl_ready, 0), False, True, True)

            pe.wait_ge(lo_ready, U_GATES + 1)
            s = U_GATES % DEPTH
            for kt in range(KT):
                o = 2 * H * kt
                mm = three(bank[6][:, :], (wh[:, s, o:o + P], wl[:, s, o:o + P]),
                           (xh[:, kt, :], xl[:, kt, :]), kt == 0, kt == KT - 1)
            mm.then_inc(g_mm, 1)

            def forget_down():
                pe.wait_ge(g_sb, 1)
                pe.wait_ge(row_ready, 1)
                pe.matmul(bank[5][0:H, :], ident[0:2 * H, H:2 * H], dw[0:2 * H, 0:S],
                          start=True, stop=True).then_inc(g_tr, 1)

            def columns_across():
                pe.wait_ge(c_sb, 1)
                for i in range(BLOCKS + TT):
                    tr = pe.transpose(bank[6][:, H * i:H * (i + 1)], column_source(i), ident[0:H, 0:H])
                tr.then_inc(c_tr, 1)

            def column_source(i):
                if i < TT:
                    return tmp[0:H, 0, i * P:(i + 1) * P]
                if i < BLOCKS:
                    o = pair_at(i - TT)
                    return dw[0:H, o:o + P]
                return tmp[0:H, 1, (i - BLOCKS) * P:(i - BLOCKS + 1) * P]

            for j in range(8):
                unit(U_O0 + j, G_O0, X, (2 * j, 2 * j + 1), None, j == 0, j == 7, inc=5 if j == 0 else 1)
                if j == 1:
                    forget_down()
                if j == 5:
                    columns_across()
            group(U_Q0, G_Q0)
            group(U_K0, G_K0)

            def R(h):
                pe.wait_ge(sel_ready, h + 1)
                if h:
                    pe.wait_ge(d_ready, h)
                pe.matmul(bank[4][:, :], nsel[:, h % 2, :], ml, start=True, stop=True).then_inc(r_mm, 1)

            def scores(h):
                i, hl = h % HH, h % HH
                pe.wait_ge(qk_l, 8 * (h // HH + 1))
                if h:
                    pe.wait_ge(n_read, h)
                else:
                    pe.wait_ge(c_ready, 1)
                if h >= 2:
                    pe.wait_ge(cell_ready, h - (h % HH > 0))
                for j in range(TT):
                    k = (kh[:, hl, j * P:(j + 1) * P], kl[:, hl, j * P:(j + 1) * P])
                    q = (qh[:, hl, j * P:(j + 1) * P], ql[:, hl, j * P:(j + 1) * P])
                    mm = three(bank[5][:, j * P:(j + 1) * P], k, q, True, True)
                mm.then_inc(s_mm, 1)
                for j, b, c in ((0, 6, 0), (1, 7, 0), (2, 7, 2 * P)):
                    n = (TT - 1 - j) * P
                    k = (kh[:, hl, j * P:(j + 1) * P], kl[:, hl, j * P:(j + 1) * P])
                    q = (qh[:, hl, (j + 1) * P:S], ql[:, hl, (j + 1) * P:S])
                    mm = three(bank[b][:, c:c + n], k, q, True, True)
                    if j != 1:
                        mm.then_inc(s_mm, 1)

            def cells(h):
                pe.wait_ge(p_l, 3 * (h + 1))
                if h % HH == 0:
                    pe.wait_ge(tile_read, NT * ((G_V1 if h else G_V0) + 1))
                for t in range(TT):
                    out = bank[5][:, 130 * t:130 * (t + 1)] if t < 3 else bank[6][:, 0:130]
                    for j in range(t + 1):
                        o = BLOCK[j, t] * P
                        mm = three(out, (ph[:, o:o + P], pl[:, o:o + P]),
                                   (vh[:, j, h % HH, :], vl[:, j, h % HH, :]), j == 0, j == t)
                mm.then_inc(n_mm, 1)

            def turn(h):
                pe.wait_ge(cn_ready, h + 1)
                pe.wait_ge(p_f, 3 * min(h + 2, HH * (h // HH + 1)))
                for t in range(TT):
                    tr = pe.transpose(bank[7][:, t * P:(t + 1) * P], cn[:, t * P:(t + 1) * P], ident[:, :])
                tr.then_inc(tr_mm, 1)

            def half(b, h0, u1, g1, u2, g2, tokens_out):
                steps = {2: lambda: R(h0)}
                for i in range(HH):
                    steps[3 + 2 * i] = lambda h=h0 + i, more=i + 1 < HH: (scores(h), R(h + 1) if more else None)
                    steps[4 + 2 * i] = lambda h=h0 + i, t=i > 0: (turn(h - 1) if t else None, cells(h))
                steps[4 + 2 * HH] = lambda: turn(h0 + HH - 1)
                group(u1, g1, after={j: f for j, f in steps.items() if j < 8})
                group(u2, g2, tokens_out=tokens_out, after={j - 8: f for j, f in steps.items() if j >= 8})

            half(0, 0, U_O1, G_O1, U_V1, G_V1, True)
            group(U_Q1, G_Q1)
            group(U_K1, G_K1)
            half(1, HH, U_U0, G_U0, U_U1, G_U1, False)

            def pool_unit(u, g_, src, need):
                pe.wait_ge(lo_ready, u + 1)
                pe.wait_ge(pool_l, need)
                s = u % DEPTH
                for n in range(NT):
                    out = claim(g_, n)
                    for k in range(2):
                        c = 512 * (n // 2) + 256 * k + P * (n % 2)
                        kt = 2 * (n // 2) + k
                        mm = three(out[:, :], (wh[:, s, c:c + P], wl[:, s, c:c + P]),
                                   (src[0][:, kt, :], src[1][:, kt, :]), k == 0, k == 1)
                    mm.then_inc(pieces, 1)

            pe.wait_ge(cell_ready, H)
            pool_unit(U_POOL0, G_POOL0, (qh, ql), NT)
            need = (xl_ready, XL_MIX)
            pooled = (tile_read, NT * G_POOL0 - H)
            for j in range(4):
                unit(U_OUT0A + j, G_OUT, X, (2 * j, 2 * j + 1), need, j == 0, False)
            pool_unit(U_POOL1, G_POOL1, (kh, kl), 2 * NT)
            for j in range(4):
                unit(U_OUT0B + j, G_OUT, X, (8 + 2 * j, 9 + 2 * j), pooled, False, j == 3)
            for i in range(3):
                group(U_OUT1 + 8 * i, G_OUT + 1 + i)
            pe.wait_ge(tile_read, NT * (G_OUT + 3))
            pe.wait_ge(ss_ready, SQ_MIX[1] + KT)
            stat(3, ssq)
            pe.wait_ge(row_ready, 2)

            with pe.Fori(0, CHUNKS) as c:
                for k in range(2 + NT):
                    for j in range(8 if k < 2 else 4):
                        l = 8 * k + j if k < 2 else 16 + 4 * (k - 2) + j
                        s = (U_FF + l) % DEPTH
                        last = j == (7 if k < 2 else 3)
                        pe.wait_ge(lo_ready, FF_UNITS * c + (U_FF + l + 1))
                        if k < 2:
                            src, need_ = X, (xl_ready, XL_FF + 2 * j + 2)
                        else:
                            src, need_ = (hidh, hidl), (hid_l, HT * c + (2 * j + 2))
                        pe.wait_ge(*need_)
                        b = banks_of(G_FF + k)
                        for n in range(NT):
                            if j == 0:
                                pe.wait_ge(tile_read, NT * 6 * c + (NT * (G_FF + k - 2) + n + 1))
                            for kk in range(2):
                                kt = 2 * j + kk
                                o = S * kk + n * P
                                mm = three(bank[b + n][:, :], (wh[:, s, o:o + P], wl[:, s, o:o + P]),
                                           (src[0][:, kt, :], src[1][:, kt, :]),
                                           j == 0 and kk == 0, last and kk == 1)
                            mm.then_inc(pieces, 1)
            for i in range(2):
                for n in range(NT):
                    held[banks_of(G_PLE - 2 + i) + n] = NT * (G_PLE - 2 + i) + n

            pe.wait_ge(tile_read, NT * (G_PLE - 1) + 3)
            pe.wait_ge(ss_ready, SQ_H[1] + KT)
            stat(6, ssq)
            pe.wait_ge(p_copied, 2)
            for i in range(4):
                if i == 2:
                    pe.wait_ge(ss_ready, SQ_FF[1] + KT)
                    pe.wait_ge(tile_read, NT * G_PLE)
                    stat(7, ssq2)
                    pe.wait_ge(ffrow, 1)
                if i == 3:
                    pe.wait_ge(ffrow_v, 1)
                unit(U_PLE + i, G_PLE + i, X, (KT - 2, KT - 1), None, True, True, inc=5 if i == 0 else 1,
                     busy=(3, ffrow_v) if i == 2 else None)

            need = (xl_ready, XL_GATE)
            group(U_GATE, G_GATE, need)
            pe.wait_ge(tile_read, NT * G_GATE)
            pe.wait_ge(ss_ready, SQ_G[1] + KT)
            stat(3, ssq)
            pe.wait_ge(row_ready, 3)
            for i in range(3):
                group(U_GATE + 8 * (i + 1), G_GATE + 1 + i)
            pe.wait_ge(tile_read, NT * (G_GATE + 3))
            pe.wait_ge(ss_ready, SQ_END[1] + KT)
            stat(4, ssq2)

        @block.scalar
        def _(act):
            link = linker(act, act_chain)

            def split(u):
                act.wait_ge(raw_in[u % DEPTH], 16 * (u // DEPTH + 1))
                if u >= DEPTH:
                    act.wait_ge(pieces, 4 * (u - DEPTH + 1))
                act.activation(wh[:, u % DEPTH, :], raw[:, u % DEPTH, :], ACT.Copy).then_inc(hi_ready, 1)

            def done(u, n):
                act.wait_ge(pieces, 4 * u + n + 1)

            def square(src, base, kt):
                if kt >= 2:
                    act.wait_ge(ss_ready, base[1] + kt - 1)
                act.activation(tmp[:, kt % 2, :], src, ACT.Square).then_inc(sq_ready, 1)

            def square_h(base, kt):
                if kt == 0:
                    act.activation(ssq[:, :], hb[:, 0, :], ACT.Square).then_inc(ss_ready, 1)
                else:
                    if kt >= 3:
                        act.wait_ge(ss_ready, base[1] + kt - 1)
                    act.activation(tmp[:, kt % 2, :], hb[:, kt, :], ACT.Square).then_inc(sq_ready, 1)

            def inverse_rms(dst, src, n=1.0 / D):
                link(act.activation(dst, src, ACT.Ln, scale=n, bias=eps[:, :]))
                return act.activation(dst, dst, ACT.Exp, scale=-0.5)

            act.wait_ge(par_in, 16)
            split(0)
            for j in range(8):
                act.wait_ge(x_in[j], 16)
                for kt in (2 * j, 2 * j + 1):
                    act.activation(xh[:, kt, :], hb[:, kt, :], ACT.Copy,
                                   scale=g(C_MIX_PRE, kt)).then_inc(xh_ready, 1)
                if j:
                    split(j)
                for kt in (2 * j, 2 * j + 1):
                    square(hb[:, kt, :], SQ_X, kt)

            def stat_x():
                act.wait_ge(consts, 4)
                act.wait_ge(stat_mm, 1)
                link(inverse_rms(row[:, :], bank[4][:, :]))
                inverse_rms(tokf[:, :], bank[5][:, 0:2 * TT:2]).then_inc(row_ready, 1)

            def v_high(u):
                act.wait_ge(row_ready, 1)
                if u > U_V0 + 7:
                    act.wait_ge(n_mm, HH)
                for t in range(TT):
                    done(u, t)
                    act.activation(vh[:, t, :, 0:P], bank[t][:, :].rearrange("p (h d) -> p h d", h=HH),
                                   ACT.Copy, scale=tokf[:, t:t + 1]).then_inc(vh_ready, 1)

            def forget_ln():
                act.wait_ge(g_x, 1)
                link(act.activation(dw[0:H, 0:S], tmp[0:H, 1, :], ACT.Abs))
                link(act.activation(dw[0:H, 0:S], dw[0:H, 0:S], ACT.Exp, scale=-1.0))
                act.activation(dw[0:H, 0:S], dw[0:H, 0:S], ACT.Ln, bias=1.0).then_inc(g_ln, 1)

            def floor_exp():
                act.wait_ge(c_ready, 1)
                act.activation(colt[:, BLOCKS:, :], colt[:, BLOCKS:, :], ACT.Exp).then_inc(em_ready, 1)

            def sigmoid_o(b):
                for n in range(NT):
                    act.wait_ge(tile_read, NT * (G_O1 if b else G_O0) + n + 1)
                    act.activation(hb[:, HH * b + n, :], hb[:, HH * b + n, :], ACT.Sigmoid).then_inc(sig_ready, 1)

            def silu(i):
                dst = (qh, kh)[(i // NT) % 2]
                act.wait_ge(y_ready, i + 1)
                if i >= 2:
                    act.wait_ge(qk_l, i - 1)
                act.activation(tmp[:, i % 2, :], dw[:, S * (i % 2):S * (i % 2) + S], ACT.Silu).then_inc(qk_f, 1)
                act.wait_ge(qk_f, i + 1)
                act.activation(dst[:, i % NT, :], tmp[:, i % 2, :], ACT.Copy).then_inc(qk_h, 1)

            def exps(h):
                act.wait_ge(diag_ready, h + 1)
                for j in range(TT):
                    act.activation(dw[:, j * P:(j + 1) * P], dw[:, j * P:(j + 1) * P], ACT.Exp,
                                   bias=colt[:, j, h:h + 1])
                for i, (j, t) in enumerate(OFF):
                    o = (TT + i) * P
                    e = act.activation(dw[:, o:o + P], bank[4][:, t * P:(t + 1) * P], ACT.Exp,
                                       bias=colt[:, TT + i, h:h + 1])
                e.then_inc(d_ready, 1)

            def p_high(h):
                for i, (a, b) in enumerate(P_PARTS):
                    act.wait_ge(p_f, 3 * h + i + 1)
                    if h:
                        act.wait_ge(n_mm, h)
                    act.activation(ph[:, a:b], dw[:, a:b], ACT.Copy).then_inc(p_h, 1)

            def cell_scale(h):
                act.wait_ge(cs_ready, h + 1)
                inverse_rms(crs[:, :], cssq[:, :], 1.0 / P).then_inc(cr_ready, 1)

            def pool_high(i):
                dst = (qh, kh)[i // NT]
                act.wait_ge(pool_f, i + 1)
                act.activation(dst[:, i % NT, :], tmp[:, i % 2, :], ACT.Copy).then_inc(pool_h, 1)

            def cell_high(kt):
                act.wait_ge(cell_ready, kt + 1)
                act.activation(xh[:, kt, :], hb[:, kt, :], ACT.Copy).then_inc(xh_ready, 1)

            def pooled_high(b, u):
                for n in range(NT):
                    done(u, n)
                    act.activation(xh[:, 8 + NT * b + n, :], bank[4 + n][:, :], ACT.Copy,
                                   scale=g(C_POOL, NT * b + n)).then_inc(xh_ready, 1)

            def mix_squares(i):
                for n in range(NT):
                    act.wait_ge(tile_read, NT * (G_OUT + i) + n + 1)
                    square(acc[:, NT * i + n, :], SQ_MIX, NT * i + n)

            def post_high(stage, kt, col):
                act.wait_ge(h_ready, KT * (stage - 2) + kt + 1)
                act.activation(xh[:, kt, :], hb[:, kt, :], ACT.Copy, scale=g(col, kt)).then_inc(xh_ready, 1)

            def row_stat(n_stat, dst, b):
                act.wait_ge(stat_mm, n_stat)
                return inverse_rms(dst, bank[b][:, :])

            during = {u: [] for u in range(UNITS)}
            before = {u: [] for u in range(UNITS)}

            def at(u, f, *args, first=False):
                (before if first else during)[u].append(lambda: f(*args))

            at(U_V0 + 6, stat_x)
            at(U_V0 + 7, v_high, U_V0 + 7)
            at(U_O0 + 2, forget_ln)
            at(U_O0 + 6, floor_exp)
            at(U_Q0, sigmoid_o, 0)
            for b, (uk, uo) in enumerate(((U_K0, U_O1), (U_K1, U_U0))):
                for n in range(NT):
                    at(uk + n, silu, 8 * b + n)
                for n in range(NT):
                    at(uo + n * 3 // 4, silu, 8 * b + NT + n)
                h0 = HH * b
                at(uo + 3, exps, h0)
                for i in range(HH):
                    at(uo + 4 + 2 * i, p_high, h0 + i)
                    if i + 1 < HH:
                        at(uo + 4 + 2 * i, exps, h0 + i + 1)
                    at(uo + 5 + 2 * i, cell_scale, h0 + i)
            at(U_O1 + 12, sigmoid_o, 1)
            at(U_V1 + 7, v_high, U_V1 + 7)
            for n in range(NT):
                at(U_U1 + 5 + n // 2, pool_high, n)
            for kt in range(H):
                at(U_POOL0, cell_high, kt, first=True)
            before[U_POOL0].insert(0, lambda: act.wait_ge(pieces, 4 * U_POOL0))
            at(U_POOL0, pooled_high, 0, U_POOL0)
            for n in range(NT):
                at(U_OUT0A + 1 + n // 2, pool_high, NT + n)
            at(U_POOL1, pooled_high, 1, U_POOL1)
            for i in range(3):
                at(U_OUT0B + 8 * i + 4, mix_squares, i)
            at(U_OUT1 + 23, mix_squares, 3)

            for u in range(5, U_FF):
                for f in before[u]:
                    f()
                split(u + LEAD)
                for f in during[u]:
                    f()

            row_stat(2, row[:, :], 3).then_inc(row_ready, 1)

            def hidden(c, j):
                t = HT * c + j
                act.wait_ge(tile_read, 6 * NT * c + (NT * G_FF + j + 1))
                r = tmp[:, j % 2, :]
                act.activation(r, r, ACT.Square).then_inc(ff_sq, 1)
                act.wait_ge(ff_sq, t + 1)
                act.activation(hidh[:, j, :], r, ACT.Copy).then_inc(hid_h, 1)

            def chunk(c, during):
                for l in range(FF_UNITS):
                    u = U_FF + l + LEAD
                    if l < 8:
                        during(l)
                    act.wait_ge(raw_in[u % DEPTH], 16 * FF_UNITS // DEPTH * c + 16 * (u // DEPTH + 1))
                    act.wait_ge(pieces, 4 * FF_UNITS * c + 4 * (u - DEPTH + 1))
                    act.activation(wh[:, u % DEPTH, :], raw[:, u % DEPTH, :], ACT.Copy).then_inc(hi_ready, 1)
                    if l in (8, 16):
                        for n in range(NT):
                            hidden(c, NT * (l // 8 - 1) + n)
                    if l < 8:
                        during(l + 0.5)
                    elif l > 16:
                        during(l)

            def first_chunk(l):
                k = int(l)
                for kt in (2 * k, 2 * k + 1):
                    if k >= 8:
                        return
                    if l == k:
                        post_high(2, kt, C_FF_PRE)
                    else:
                        square_h(SQ_H, kt)

            def ff_squares(i):
                for n in range(NT):
                    act.wait_ge(tile_read, NT * (G_PLE - NT + i) + n + 1)
                    square(acc[:, NT * i + n, :], SQ_FF, NT * i + n)

            def last_chunk(l):
                if l in (20, 24, 28):
                    ff_squares(int(l) // 4 - 5)

            chunk(0, first_chunk)
            with act.Fori(1, CHUNKS - 1) as c:
                chunk(c, lambda l: None)
            chunk(CHUNKS - 1, last_chunk)

            ff_squares(NT - 1)
            split(U_P + LEAD)
            act.wait_ge(stat_mm, 3)
            act.activation(row[:, :], bank[6][:, :], ACT.Ln, scale=1.0 / D, bias=eps[:, :]).then_inc(ffrow, 1)
            act.wait_ge(ffrow, 1)
            act.wait_ge(ss_ready, SQ_FF[1] + KT)
            act.activation(tmp[:, 0, :], row[:, :], ACT.Exp, scale=-2.0).then_inc(ffrow, 1)
            split(U_PLE + LEAD)
            split(U_PLE + 1 + LEAD)
            act.wait_ge(ffrow_v, 1)
            act.activation(tmp[:, 1, :], tmp[:, 0, :], ACT.Ln, bias=eps[:, :]).then_inc(ffrow, 1)
            act.wait_ge(ffrow_v, 2)
            act.activation(row[:, :], tmp[:, 0, :], ACT.Exp, scale=-1.0).then_inc(ffrow, 1)
            split(U_PLE + 2 + LEAD)
            split(U_PLE + 3 + LEAD)

            def sigmoid_gate(i, n):
                m = NT * i + n
                act.wait_ge(tile_read, NT * (G_GATE + i) + n + 1)
                act.activation(acc[:, m, :], acc[:, m, :], ACT.Sigmoid).then_inc(gsig, 1)

            def final_square(m):
                act.wait_ge(prod_ready, m + 1)
                square(acc[:, m, :], SQ_END, m)
                act.activation(acc[:, m, :], acc[:, m, :], ACT.Copy, scale=g(C_PLE_POST, m)).then_inc(fin_g, 1)

            def gate_group(i):
                for n in range(NT):
                    sigmoid_gate(i, n)
                    if n:
                        final_square(NT * i + n - 1)
                final_square(NT * i + NT - 1)

            for u in range(U_GATE, UNITS):
                j = u - U_GATE
                if j < 8:
                    post_high(3, 2 * j, C_PLE_GATE)
                    post_high(3, 2 * j + 1, C_PLE_GATE)
                if u + LEAD < UNITS:
                    split(u + LEAD)
                if j < 8:
                    square_h(SQ_G, 2 * j)
                    square_h(SQ_G, 2 * j + 1)
                if j == 8:
                    row_stat(5, row[:, :], 3).then_inc(row_ready, 1)
                if j in (9, 17, 25):
                    gate_group((j - 9) // 8)
            gate_group(3)
            row_stat(6, row[:, :], 4).then_inc(row_ready, 1)
            ov = out_t.rearrange("(k p) t -> k p t", p=P)
            for i, m in enumerate(POOL_TILES):
                act.wait_ge(out_g, i + 1)
                act.dma_start(ov[m], hb[:, m, :]).then_inc(stored, 16)

        @block.vector
        def _(dve):
            link = linker(dve, dve_chain)

            def done(u, n):
                dve.wait_ge(pieces, 4 * u + n + 1)

            def add_square(dst, base, kt):
                dve.wait_ge(sq_ready, base[0] + kt + 1)
                if kt == 0:
                    dve.tensor_copy(dst[:, :], tmp[:, 0, :]).then_inc(ss_ready, 1)
                else:
                    dve.wait_ge(ss_ready, base[1] + kt)
                    dve.tensor_tensor(dst[:, :], dst[:, :], tmp[:, kt % 2, :], ALU.add).then_inc(ss_ready, 1)

            link(*[dve.memset(vh[:, t, :, P:P + 1].bitcast(F32), 1.0) for t in range(TT)],
                 *[dve.memset(vh[:, t, :, P + 1:P + 2].bitcast(F32), 0.0) for t in range(TT)],
                 *[dve.memset(vl[:, t, :, P:P + 2].bitcast(F32), 0.0) for t in range(TT)],
                 *[dve.memset(win[:, t:t + 1], 1.0 / (t + 1)) for t in range(16)])

            dve.wait_ge(par_in, 16)
            for j in range(8):
                dve.wait_ge(x_in[j], 16)
                for kt in (2 * j, 2 * j + 1):
                    dve.wait_ge(xh_ready, kt + 1)
                    dve.scalar_tensor_tensor(out=xl[:, kt, :], in0=hb[:, kt, :], scalar=g(C_MIX_PRE, kt),
                                             in1=xh[:, kt, :].bitcast(F32), op0=ALU.mult,
                                             op1=ALU.subtract).then_inc(xl_ready, 1)
                for kt in (2 * j, 2 * j + 1):
                    add_square(ssq, SQ_X, kt)

            def v_low(b, u):
                for t in range(TT):
                    dve.wait_ge(vh_ready, NT * b + t + 1)
                    shape = bank[t][:, :].rearrange("p (h d) -> p h d", h=HH)
                    dve.scalar_tensor_tensor(out=vl[:, t, :, 0:P], in0=shape, scalar=tokf[:, t:t + 1],
                                             in1=vh[:, t, :, 0:P].bitcast(F32), op0=ALU.mult,
                                             op1=ALU.subtract).then_inc(tile_read, 1)

            def scaled(u, at_tile):
                for n in range(NT):
                    done(u, n)
                    dve.tensor_tensor(hb[:, at_tile + n, :], bank[n][:, :], row[:, :],
                                      ALU.mult).then_inc(tile_read, 1)

            v_low(0, U_V0 + 7)

            dve.wait_ge(g_mm, 1)
            dve.tensor_tensor(dw[0:2 * H, 0:S], bank[6][0:2 * H, :], row[0:2 * H, :], ALU.mult).then_inc(g_sb, 1)
            gi, fg = tmp[0:H, 0, :], tmp[0:H, 1, :]
            dve.wait_ge(g_sb, 1)
            link(dve.tensor_scalar(gi, dw[0:H, 0:S], par[0:H, C_BIAS:C_BIAS + 1], None, ALU.add))
            dve.wait_ge(g_tr, 1)
            dve.tensor_scalar(fg, bank[5][0:H, :], par[0:H, C_BIAS + 1:C_BIAS + 2], None,
                              ALU.add).then_inc(g_x, 1)
            dve.wait_ge(g_x, 1)
            dve.wait_ge(g_ln, 1)
            link(dve.scalar_tensor_tensor(out=fg, in0=fg, scalar=0.0, in1=dw[0:H, 0:S],
                                          op0=ALU.min, op1=ALU.subtract))
            bb = dw[0:H, S:2 * S]
            for t in range(TT):
                o = slice(t * P, (t + 1) * P)
                e = dve.tensor_tensor_scan(bb[:, o], ones[0:H, :], fg[:, o], 0.0, ALU.mult, ALU.add)
                link(e)
            link(dve.tensor_tensor(gi, gi, bb, ALU.subtract))
            for t in range(TT):
                o = slice(t * P, (t + 1) * P)
                link(dve.tensor_tensor_scan(ml[:, o], gi[:, o], gi[:, o], mp[:, t:t + 1] if t else 0.0,
                                            ALU.max, ALU.max))
                if t + 1 < TT:
                    e = (t + 1) * P
                    link(dve.tensor_tensor(mp[:, t + 1:t + 2], ml[:, e - 1:e], bb[:, e - 1:e], ALU.add))
            link(dve.tensor_tensor(fg, bb, ml, ALU.add))
            link(dve.tensor_scalar(fg, fg, -1.0, EXP_MAX, ALU.mult, ALU.min))
            for i, (j, t) in enumerate(OFF):
                o, e = pair_at(i), t * P
                src = gi[:, j * P:(j + 1) * P] if t == j + 1 else dw[0:H, pair_at(i - 1):pair_at(i - 1) + P]
                ins = dve.tensor_scalar(dw[0:H, o:o + P], src, bb[:, e - 1:e], None, ALU.add)
                if i + 1 < len(OFF):
                    link(ins)
            ins.then_inc(c_sb, 1)
            dve.wait_ge(c_tr, 1)
            dve.tensor_copy(colt[:, :, :], bank[6][:, 0:H * (BLOCKS + TT)].rearrange(
                "p (i h) -> p i h", h=H)).then_inc(c_ready, 1)

            scaled(U_O0 + 7, 0)

            def conv(i, tile, wtile):
                y = dw[:, S * (i % 2):S * (i % 2) + S]
                x = hb[:, tile, :]

                def w(k):
                    return par[:, C_CONV + CONV * wtile + k:C_CONV + CONV * wtile + k + 1]
                link(dve.tensor_scalar(y, x, w(CONV - 1), None, ALU.mult))
                for s in range(1, CONV):
                    ins = dve.scalar_tensor_tensor(out=y[:, s:], in0=x[:, :S - s], scalar=w(CONV - 1 - s),
                                                   in1=y[:, s:], op0=ALU.mult, op1=ALU.add)
                    if s < CONV - 1:
                        link(ins)
                ins.then_inc(y_ready, 1)

            def qk_low(i):
                dst, hi = ((ql, qh), (kl, kh))[(i // NT) % 2]
                dve.wait_ge(qk_h, i + 1)
                dve.tensor_tensor(dst[:, i % NT, :], tmp[:, i % 2, :], hi[:, i % NT, :].bitcast(F32),
                                  ALU.subtract).then_inc(qk_l, 1)

            def qk(b, is_k, u, g_):
                base = 8 + NT * is_k
                scaled(u + 7, base)
                dve.wait_ge(tile_read, NT * (g_ + 1))
                i0 = 8 * b + NT * is_k
                for n in range(NT):
                    conv(i0 + n, base + n, 8 * is_k + NT * b + n)
                    if n:
                        qk_low(i0 + n - 1)
                qk_low(i0 + NT - 1)

            def select(h):
                dve.tensor_scalar(nsel[:, h % 2, :], ones[0:H, :], ident[0:H, h:h + 1], -1.0,
                                  ALU.mult, ALU.mult).then_inc(sel_ready, 1)

            def diag(h):
                dve.wait_ge(r_mm, h + 1)
                if h % HH:
                    dve.wait_ge(p_l, 3 * h)
                dve.tensor_tensor(dw[:, 0:S].rearrange("p (t n) -> p t n", t=TT),
                                  bank[4][:, :].rearrange("p (t n) -> p t n", t=TT),
                                  mask[:, :].unsqueeze(1).to_broadcast([P, TT, P]),
                                  ALU.add).then_inc(diag_ready, 1)

            def weigh(h):
                dve.wait_ge(d_ready, h + 1)
                for i, (a, b) in enumerate(P_PARTS):
                    dve.wait_ge(s_mm, 3 * h + i + 1)
                    dve.scalar_tensor_tensor(out=dw[:, a:b], in0=bank[5 + i][:, 0:b - a], scalar=P ** -0.5,
                                             in1=dw[:, a:b], op0=ALU.mult, op1=ALU.mult).then_inc(p_f, 1)
                for i, (a, b) in enumerate(P_PARTS):
                    dve.wait_ge(p_h, 3 * h + i + 1)
                    dve.tensor_tensor(pl[:, a:b], dw[:, a:b], ph[:, a:b].bitcast(F32),
                                      ALU.subtract).then_inc(p_l, 1)

            def normalise(h):
                dve.wait_ge(n_mm, h + 1)
                dve.wait_ge(em_ready, 1)
                link(dve.tensor_copy(den[:, 0:3],
                                     bank[5][:, 0:390].rearrange("p (t n) -> p t n", n=130)[:, :, P]),
                     dve.tensor_copy(den[:, 3:4], bank[6][:, P:P + 1]))
                link(dve.scalar_tensor_tensor(out=den[:, :], in0=den[:, :], scalar=-1.0, in1=den[:, :],
                                              op0=ALU.mult, op1=ALU.max))
                link(dve.tensor_tensor(den[:, :], den[:, :], colt[:, BLOCKS:, h], ALU.max))
                link(dve.reciprocal(den[:, :], den[:, :]))
                for t in range(TT):
                    src = bank[5][:, 130 * t:130 * t + P] if t < 3 else bank[6][:, 0:P]
                    e = dve.tensor_scalar(cn[:, t * P:(t + 1) * P], src, den[:, t:t + 1], None, ALU.mult)
                e.then_inc(n_read, 1)
                dve.wait_ge(n_read, h + 1)
                for t in range(TT):
                    c = cn[:, t * P:(t + 1) * P]
                    e = dve.tensor_tensor_reduce(out=tmp[:, 1, t * P:(t + 1) * P], in0=c, in1=c, scale=1.0,
                                                 scalar=0.0, op0=ALU.mult, op1=ALU.add,
                                                 accum_out=cssq[:, t:t + 1])
                e.then_inc(cs_ready, 1)

            def scale_cell(h):
                dve.wait_ge(cr_ready, h + 1)
                for t in range(TT):
                    c = cn[:, t * P:(t + 1) * P]
                    e = dve.tensor_scalar(c, c, crs[:, t:t + 1], None, ALU.mult)
                e.then_inc(cn_ready, 1)

            def gate_cell(h):
                dve.wait_ge(tr_mm, h + 1)
                dve.wait_ge(sig_ready, h + 1)
                dve.scalar_tensor_tensor(out=hb[:, h, :], in0=bank[7][:, :], scalar=g(C_MLSTM, h),
                                         in1=hb[:, h, :], op0=ALU.mult, op1=ALU.mult).then_inc(cell_ready, 1)

            def half(h0, middle):
                select(h0)
                select(h0 + 1)
                diag(h0)
                for i in range(HH):
                    h = h0 + i
                    if i == 2:
                        middle()
                    if i:
                        scale_cell(h - 1)
                    weigh(h)
                    if i + 1 < HH:
                        diag(h + 1)
                        if i + 2 < HH:
                            select(h + 2)
                    if i:
                        gate_cell(h - 1)
                    normalise(h)
                scale_cell(h0 + HH - 1)
                gate_cell(h0 + HH - 1)

            qk(0, 0, U_Q0, G_Q0)
            qk(0, 1, U_K0, G_K0)
            half(0, lambda: scaled(U_O1 + 7, HH))
            v_low(1, U_V1 + 7)
            qk(1, 0, U_Q1, G_Q1)
            qk(1, 1, U_K1, G_K1)
            half(HH, lambda: scaled(U_U0 + 7, 8))

            def pooling(i):
                w = WINDOWS[i // 2]
                u = hb[:, 8 + i, :]
                src, d, flip = u, 1, 0
                if i:
                    dve.wait_ge(pool_f, i)
                while d < w:
                    dst = dw[:, S * flip:S * flip + S]
                    link(dve.tensor_copy(dst[:, 0:d], src[:, 0:d]),
                         dve.tensor_tensor(dst[:, d:], src[:, d:], src[:, :S - d], ALU.add))
                    src, d, flip = dst, 2 * d, 1 - flip
                out = tmp[:, i % 2, :]
                link(dve.tensor_tensor(out[:, 0:w - 1], src[:, 0:w - 1], win[:, 0:w - 1], ALU.mult))
                link(dve.tensor_tensor(out[:, 0:w - 1], out[:, 0:w - 1], u[:, 0:w - 1], ALU.subtract))
                dve.scalar_tensor_tensor(out=out[:, w - 1:], in0=src[:, w - 1:], scalar=1.0 / w,
                                         in1=u[:, w - 1:], op0=ALU.mult, op1=ALU.subtract).then_inc(pool_f, 1)

            def pool_low(i):
                dst, hi = ((ql, qh), (kl, kh))[i // NT]
                dve.wait_ge(pool_h, i + 1)
                dve.tensor_tensor(dst[:, i % NT, :], tmp[:, i % 2, :], hi[:, i % NT, :].bitcast(F32),
                                  ALU.subtract).then_inc(pool_l, 1)

            def pool_half(b):
                for n in range(NT):
                    pooling(NT * b + n)
                    if n:
                        pool_low(NT * b + n - 1)
                pool_low(NT * b + NT - 1)

            dve.wait_ge(tile_read, NT * (G_U0 + 1))
            pool_half(0)
            scaled(U_U1 + 7, 12)
            dve.wait_ge(cell_ready, H)
            for kt in range(H):
                dve.wait_ge(xh_ready, KT + kt + 1)
                dve.tensor_tensor(xl[:, kt, :], hb[:, kt, :], xh[:, kt, :].bitcast(F32),
                                  ALU.subtract).then_inc(xl_ready, 1)

            def pooled_low(b):
                for n in range(NT):
                    kt = 8 + NT * b + n
                    dve.wait_ge(xh_ready, KT + kt + 1)
                    dve.scalar_tensor_tensor(out=xl[:, kt, :], in0=bank[4 + n][:, :],
                                             scalar=g(C_POOL, NT * b + n), in1=xh[:, kt, :].bitcast(F32),
                                             op0=ALU.mult, op1=ALU.subtract).then_inc(tile_read, 1)

            pooled_low(0)
            dve.wait_ge(tile_read, NT * (G_POOL0 + 1))
            pool_half(1)
            pooled_low(1)

            for i in range(NT):
                u = U_OUT0B + 3 + 8 * i
                for n in range(NT):
                    done(u, n)
                    dve.tensor_copy(acc[:, NT * i + n, :], bank[banks_of(G_OUT + i) + n][:, :])\
                       .then_inc(tile_read, 1)
                    if n:
                        add_square(ssq, SQ_MIX, NT * i + n - 1)
                add_square(ssq, SQ_MIX, NT * i + NT - 1)

            def post_norm(stage, post, pre, between=None):
                def low(kt):
                    dve.wait_ge(xh_ready, KT * stage + kt + 1)
                    dve.scalar_tensor_tensor(out=xl[:, kt, :], in0=hb[:, kt, :], scalar=g(pre, kt),
                                             in1=xh[:, kt, :].bitcast(F32), op0=ALU.mult,
                                             op1=ALU.subtract).then_inc(xl_ready, 1)

                def scale(kt):
                    dve.tensor_tensor(acc[:, kt, :], acc[:, kt, :], row[:, :], ALU.mult).then_inc(scaled_acc, 1)

                scale(0)
                for kt in range(KT):
                    if between:
                        between(kt)
                    if kt >= 2 or kt == 1:
                        low(kt - 1)
                    dve.wait_ge(scaled_acc, KT * (stage - 2) + kt + 1)
                    dve.scalar_tensor_tensor(out=hb[:, kt, :], in0=acc[:, kt, :], scalar=g(post, kt),
                                             in1=hb[:, kt, :], op0=ALU.mult, op1=ALU.add).then_inc(h_ready, 1)
                    if kt + 1 < KT:
                        scale(kt + 1)
                low(KT - 1)

            dve.wait_ge(row_ready, 2)
            dve.wait_ge(xr_in, 16 * KT // 2)
            dve.wait_ge(tile_read, NT * G_FF)
            post_norm(2, C_MIX_POST, C_FF_PRE)
            link(dve.memset(acc[:, :, :], 0.0))

            def chunk(c, last=False):
                def low(j):
                    dve.wait_ge(hid_h, HT * c + (j + 1))
                    dve.tensor_tensor(hidl[:, j, :], tmp[:, j % 2, :], hidh[:, j, :].bitcast(F32),
                                      ALU.subtract).then_inc(hid_l, 1)
                for k in range(2 + NT):
                    u = U_FF + (8 * k + 7 if k < 2 else 16 + 4 * (k - 2) + 3)
                    if last and k == 5:
                        copy_p()
                    for n in range(NT):
                        b = bank[banks_of(G_FF + k) + n]
                        dve.wait_ge(pieces, 4 * FF_UNITS * c + (4 * u + n + 1))
                        if k < 2:
                            j = NT * k + n
                            if j >= 2:
                                dve.wait_ge(hid_l, HT * c + (j - 1))
                            dve.tensor_scalar(tmp[:, j % 2, :], b[:, :], 0.0, None, ALU.max)\
                               .then_inc(tile_read, 1)
                            if j:
                                low(j - 1)
                            if j == HT - 1:
                                low(j)
                        else:
                            m = NT * (k - 2) + n
                            dve.tensor_tensor(acc[:, m, :], b[:, :], acc[:, m, :], ALU.add)\
                               .then_inc(tile_read, 1)
                            if last and n:
                                add_square(ssq2, SQ_FF, m - 1)
                    if last and k >= 2:
                        add_square(ssq2, SQ_FF, NT * (k - 2) + NT - 1)

            def copy_p():
                dve.wait_ge(lo_ready, U_P + 1)
                s = U_P % DEPTH
                dve.tensor_copy(xh[:, KT - 2:, :], wh[:, s, :].bitcast(F32).rearrange(
                    "p (k t) -> p k t", k=2)).then_inc(p_copied, 1)
                dve.tensor_copy(xl[:, KT - 2:, :], wl[:, s, :].bitcast(F32).rearrange(
                    "p (k t) -> p k t", k=2)).then_inc(p_copied, 1)

            dve.wait_ge(ss_ready, SQ_FF[1])
            with dve.Fori(0, CHUNKS - 1) as c:
                chunk(c)
            chunk(CHUNKS - 1, last=True)

            def embedding(i):
                for n in range(NT):
                    done(U_PLE + i, n)
                    dve.tensor_copy(emb[:, NT * i + n, :], bank[banks_of(G_PLE + i) + n][:, :])\
                       .then_inc(tile_read, 1)

            embedding(0)
            embedding(1)
            dve.wait_ge(ffrow, 2)
            dve.wait_ge(stat_mm, 4)
            dve.scalar_tensor_tensor(out=tmp[:, 0, :], in0=bank[7][:, :], scalar=1.0 / D, in1=tmp[:, 0, :],
                                     op0=ALU.mult, op1=ALU.mult).then_inc(ffrow_v, 1)
            dve.wait_ge(ffrow, 3)
            dve.scalar_tensor_tensor(out=tmp[:, 0, :], in0=tmp[:, 1, :], scalar=0.5, in1=row[:, :],
                                     op0=ALU.mult, op1=ALU.add).then_inc(ffrow_v, 1)
            embedding(2)
            dve.wait_ge(ffrow, 4)
            post_norm(3, C_FF_POST, C_PLE_GATE, between=lambda kt: embedding(3) if kt == 3 else None)

            dve.wait_ge(row_ready, 3)
            for i in range(NT):
                def product(m):
                    dve.wait_ge(gsig, m + 1)
                    dve.tensor_tensor(acc[:, m, :], acc[:, m, :], emb[:, m, :], ALU.mult)\
                       .then_inc(prod_ready, 1)
                for n in range(NT + 2):
                    m = NT * i + n
                    if n < NT:
                        done(U_GATE + 8 * i + 7, n)
                        dve.tensor_tensor(acc[:, m, :], bank[banks_of(G_GATE + i) + n][:, :], row[:, :],
                                          ALU.mult).then_inc(tile_read, 1)
                    if 1 <= n <= NT:
                        product(m - 1)
                    if n >= 2:
                        add_square(ssq2, SQ_END, m - 2)
            dve.wait_ge(row_ready, 4)
            def scale(m):
                dve.wait_ge(fin_g, m + 1)
                dve.tensor_tensor(acc[:, m, :], acc[:, m, :], row[:, :], ALU.mult).then_inc(scaled_acc, 1)

            scale(VECTOR_TILES[0])
            for i, m in enumerate(VECTOR_TILES):
                if i + 1 < len(VECTOR_TILES):
                    scale(VECTOR_TILES[i + 1])
                dve.wait_ge(scaled_acc, 2 * KT + i + 1)
                dve.tensor_tensor(hb[:, m, :], hb[:, m, :], acc[:, m, :], ALU.add).then_inc(out_v, 1)


def pair_at(i):
    return i * P if i < 4 else 2 * S + (i - 4) * P


P_PARTS = [(0, S), (S, S + 3 * P), (S + 3 * P, S + 6 * P)]
VECTOR_TILES = [m for m in range(KT) if m % 3 != 1]
POOL_TILES = [m for m in range(KT) if m % 3 == 1]


def pack(w):
    k, n = w.shape
    return w.reshape(k // 256, 2, P, n // 512, 512).transpose(3, 0, 2, 1, 4).reshape(
        n // 512, k // 256, P, 1024)


def kernel(x, p, w_in, b_gates, w_qk_conv, g_mlstm, w_pool, pool_scale, w_out, g_mix_pre, g_mix_post,
           w_ff1, w_ff2, g_ff_pre, g_ff_post, w_ple_proj, w_ple_gate, g_ple_gate, g_ple_post):
    import numpy as np
    import concourse.bacc as bacc
    from concourse.bass_utils import run_bass_kernel_spmd

    a = {k: np.asarray(v)[0] for k, v in dict(
        x=x, p=np.asarray(p)[0], w_in=w_in, b_gates=b_gates, conv=w_qk_conv, g_mlstm=g_mlstm,
        w_pool=w_pool, pool_scale=pool_scale, w_out=w_out, g_mix_pre=g_mix_pre, g_mix_post=g_mix_post,
        w_ff1=w_ff1, w_ff2=w_ff2, g_ff_pre=g_ff_pre, g_ff_post=g_ff_post, w_ple_proj=w_ple_proj,
        w_ple_gate=w_ple_gate, g_ple_gate=g_ple_gate, g_ple_post=g_ple_post).items()}
    w = a["w_in"]
    m = D // 2
    q, k, v, o = (pack(w[:, i * m:(i + 1) * m]) for i in range(4))
    gates = w[:, 4 * m:4 * m + 2 * H]
    u = pack(w[:, 4 * m + 2 * H:])
    gates_u = np.zeros((1, P, 1024), np.float32)
    gates_u[0, :, 0:KT * 2 * H] = gates.reshape(KT, P, 2 * H).transpose(1, 0, 2).reshape(P, -1)
    pools = a["w_pool"].reshape(2, 2, 2, P, 256).transpose(0, 3, 1, 2, 4).reshape(2, P, 1024)
    wo = pack(a["w_out"])
    ff1 = pack(a["w_ff1"]).reshape(CHUNKS, 16, P, 1024)
    ff2 = pack(a["w_ff2"]).reshape(4, CHUNKS, 4, P, 1024).transpose(1, 0, 2, 3, 4).reshape(
        CHUNKS, 16, P, 1024)
    ff = np.concatenate([ff1, ff2], axis=1).reshape(-1, P, 1024)
    p_unit = a["p"].T.reshape(2, P, S).transpose(1, 0, 2).reshape(1, P, 1024)
    stream = np.concatenate([
        v[0], gates_u, o[0], q[0], k[0], o[1], v[1], q[1], k[1], u[0], u[1], pools[0:1], wo[0, 0:4],
        pools[1:2], wo[0, 4:8], wo[1], wo[2], wo[3], ff, p_unit,
        pack(a["w_ple_proj"]).reshape(4, P, 1024), pack(a["w_ple_gate"]).reshape(32, P, 1024)])
    assert stream.shape[0] == UNITS
    par = np.zeros((P, PARAMS), np.float32)
    for c, name in ((C_MIX_PRE, "g_mix_pre"), (C_MIX_POST, "g_mix_post"), (C_FF_PRE, "g_ff_pre"),
                    (C_FF_POST, "g_ff_post"), (C_PLE_GATE, "g_ple_gate"), (C_PLE_POST, "g_ple_post"),
                    (C_MLSTM, "g_mlstm"), (C_POOL, "pool_scale")):
        t = a[name].reshape(-1, P).T
        par[:, c:c + t.shape[1]] = t
    par[:, C_CONV:C_CONV + 16 * CONV] = a["conv"].reshape(CONV, 16, P).transpose(2, 1, 0).reshape(P, -1)
    par[0:H, C_BIAS:C_BIAS + 2] = a["b_gates"].reshape(2, H).T
    arrays = {"stream": np.ascontiguousarray(stream), "x_t": np.ascontiguousarray(a["x"].T), "params": par}

    nc = bacc.Bacc("TRN2", target_bir_lowering=False, num_devices=1, dynamic_dma_scratch_size=1024)
    aps = [nc.dram_tensor(n, arr.shape, F32, kind="ExternalInput").ap() for n, arr in arrays.items()]
    out = nc.dram_tensor("out_t", (D, S), F32, kind="ExternalOutput").ap()
    build(nc, *aps, out)
    r = run_bass_kernel_spmd(nc, [arrays], core_ids=[0])
    return np.ascontiguousarray(r.results[0]["out_t"].T)[None]
```

```python
from contextlib import ExitStack

import concourse.bass as bass
from concourse import mybir

F32 = mybir.dt.float32
F32R = mybir.dt.float32r
ALU = mybir.AluOpType
ACT = mybir.ActivationFunctionType

P = 128
S = 512
D = 2048
KT = D // P
H = 8
HH = H // 2
TT = S // P
NT = 4
CONV = 4
WINDOWS = (2, 4, 8, 16)
EPS = 1e-6
FF = 4 * D
CHUNKS = 8
HT = FF // CHUNKS // P
DEPTH = 4
LEAD = DEPTH - 1

U_V0 = 0
U_GATES = U_V0 + 8
U_O0 = U_GATES + 1
U_Q0 = U_O0 + 8
U_K0 = U_Q0 + 8
U_O1 = U_K0 + 8
U_V1 = U_O1 + 8
U_Q1 = U_V1 + 8
U_K1 = U_Q1 + 8
U_U0 = U_K1 + 8
U_U1 = U_U0 + 8
U_POOL0 = U_U1 + 8
U_OUT0A = U_POOL0 + 1
U_POOL1 = U_OUT0A + 4
U_OUT0B = U_POOL1 + 1
U_OUT1 = U_OUT0B + 4
U_FF = U_OUT1 + 24
FF_UNITS = 32
U_P = U_FF + CHUNKS * FF_UNITS
U_PLE = U_P + 1
U_GATE = U_PLE + 4
UNITS = U_GATE + 32

(G_V0, G_O0, G_Q0, G_K0, G_O1, G_V1, G_Q1, G_K1, G_U0, G_U1, G_POOL0, G_POOL1, G_OUT) = range(13)
G_FF = G_OUT + 4
G_PLE = G_FF + 6 * CHUNKS
G_GATE = G_PLE + 3
G_EMB3 = G_GATE + 4

C_MIX_PRE, C_MIX_POST, C_FF_PRE, C_FF_POST, C_PLE_GATE, C_PLE_POST = (KT * i for i in range(6))
C_MLSTM = 6 * KT
C_POOL = C_MLSTM + H
C_CONV = C_POOL + 8
C_BIAS = C_CONV + 16 * CONV
PARAMS = C_BIAS + 2

OFF = [(0, 1), (0, 2), (0, 3), (1, 2), (1, 3), (2, 3)]
SOURCES = [(0, 0), (1, TT), (3, 2 * TT - 1), (2, 2 * TT)]
BLOCK = {(j, t): o + t - j for j, o in SOURCES for t in range(j, TT)}
BLOCKS = len(BLOCK)
NEG = -1e30
XL_MIX = KT
XL_FF = XL_MIX + H
XL_GATE = XL_FF + KT
SQ_X, SQ_MIX, SQ_H, SQ_FF, SQ_G, SQ_END = ((0, 0), (16, 16), (32, 30), (48, 45), (64, 59), (80, 74))
EXP_MAX = 88.0


def banks_of(g):
    if g in (G_POOL0, G_POOL1):
        return 4
    if g < G_OUT:
        return 0
    if g == G_EMB3:
        return 0
    if G_PLE <= g < G_GATE:
        return 4 if g == G_PLE + 2 else 0
    if g >= G_GATE:
        return 4 * ((g - G_GATE + 1) % 2)
    return 4 * ((g - G_OUT) % 2)


def build(nc, stream, x_t, params, out_t):
    ctx = ExitStack()
    with ctx:
        def sem(name):
            return ctx.enter_context(nc.semaphore(name))

        def sb(name, shape, dt=F32, stack=ctx):
            return stack.enter_context(nc.sbuf_tensor(name, shape, dt))

        hb = sb("hb", [P, KT, S])
        xh = sb("xh", [P, KT, S], F32R)
        xl = sb("xl", [P, KT, S], F32R)
        raw = sb("raw", [P, DEPTH, 1024])
        wh = sb("wh", [P, DEPTH, 1024], F32R)
        wl = sb("wl", [P, DEPTH, 1024], F32R)
        tmp = sb("tmp", [P, 2, S])
        row = sb("row", [P, S])
        ssq = sb("ssq", [P, S])
        ident = sb("ident", [P, P])
        ones = sb("ones", [P, P])
        mask = sb("mask", [P, P])
        par = sb("par", [P, PARAMS])
        eps = sb("eps", [P, 1])
        win = sb("win", [P, 16])
        tokf = sb("tokf", [P, TT])
        colt = sb("colt", [P, BLOCKS + TT, H])
        mp = sb("mp", [H, TT])
        nsel = sb("nsel", [H, 2, P])
        den = sb("den", [P, TT])
        cssq = sb("cssq", [P, TT])
        crs = sb("crs", [P, TT])
        mixer = ExitStack()
        with mixer:
            vh = sb("vh", [P, TT, HH, 130], F32R, mixer)
            vl = sb("vl", [P, TT, HH, 130], F32R, mixer)
            qh = sb("qh", [P, HH, S], F32R, mixer)
            ql = sb("ql", [P, HH, S], F32R, mixer)
            kh = sb("kh", [P, HH, S], F32R, mixer)
            kl = sb("kl", [P, HH, S], F32R, mixer)
            dw = sb("dw", [P, BLOCKS * P], F32, mixer)
            ph = sb("ph", [P, BLOCKS * P], F32R, mixer)
            pl = sb("pl", [P, BLOCKS * P], F32R, mixer)
        acc = sb("acc", [P, KT, S])
        hid_stack = ExitStack()
        with hid_stack:
            hidh = sb("hidh", [P, HT, S], F32R, hid_stack)
            hidl = sb("hidl", [P, HT, S], F32R, hid_stack)
        emb = sb("emb", [P, KT, S])
        ssq2 = sb("ssq2", [P, S])
        ml = ssq[0:H, :]
        cn = tmp[:, 0, :]

        bank = [ctx.enter_context(nc.psum_tensor(f"bank{i}", [P, 512], F32)) for i in range(8)]

        x_in = [sem(f"x_in{j}") for j in range(KT // 2)]
        par_in = sem("par_in")
        xr_in = sem("xr_in")
        raw_in = [sem(f"raw_in{s}") for s in range(DEPTH)]
        hi_ready = sem("hi_ready")
        lo_ready = sem("lo_ready")
        pieces = sem("pieces")
        tile_read = sem("tile_read")
        consts = sem("consts")
        xh_ready = sem("xh_ready")
        xl_ready = sem("xl_ready")
        sq_ready = sem("sq_ready")
        ss_ready = sem("ss_ready")
        stat_mm = sem("stat_mm")
        row_ready = sem("row_ready")
        vh_ready = sem("vh_ready")
        g_mm = sem("g_mm")
        g_sb = sem("g_sb")
        g_tr = sem("g_tr")
        g_ln = sem("g_ln")
        g_x = sem("g_x")
        c_sb = sem("c_sb")
        c_tr = sem("c_tr")
        c_ready = sem("c_ready")
        em_ready = sem("em_ready")
        sig_ready = sem("sig_ready")
        y_ready = sem("y_ready")
        qk_f = sem("qk_f")
        qk_h = sem("qk_h")
        qk_l = sem("qk_l")
        sel_ready = sem("sel_ready")
        r_mm = sem("r_mm")
        diag_ready = sem("diag_ready")
        d_ready = sem("d_ready")
        s_mm = sem("s_mm")
        p_f = sem("p_f")
        p_h = sem("p_h")
        p_l = sem("p_l")
        n_mm = sem("n_mm")
        n_read = sem("n_read")
        cs_ready = sem("cs_ready")
        cr_ready = sem("cr_ready")
        cn_ready = sem("cn_ready")
        tr_mm = sem("tr_mm")
        cell_ready = sem("cell_ready")
        pool_f = sem("pool_f")
        pool_h = sem("pool_h")
        pool_l = sem("pool_l")
        h_ready = sem("h_ready")
        scaled_acc = sem("scaled_acc")
        hid_h = sem("hid_h")
        hid_l = sem("hid_l")
        ff_sq = sem("ff_sq")
        p_copied = sem("p_copied")
        emb_read = sem("emb_read")
        ffrow = sem("ffrow")
        ffrow_v = sem("ffrow_v")
        gsig = sem("gsig")
        prod_ready = sem("prod_ready")
        fin_g = sem("fin_g")
        dve_chain = sem("dve_chain")
        act_chain = sem("act_chain")
        pool_chain = sem("pool_chain")
        out_v = sem("out_v")
        out_g = sem("out_g")
        out_a = sem("out_a")
        y_scaled = sem("y_scaled")
        sum_mm = sem("sum_mm")
        stored = sem("stored")

        block = ctx.enter_context(nc.Block())

        def linker(eng, chain):
            count = [0]

            def link(*instructions):
                for ins in instructions:
                    ins.then_inc(chain, 1)
                count[0] += len(instructions)
                eng.wait_ge(chain, count[0])
            return link

        def g(col, kt):
            return par[:, col + kt:col + kt + 1]

        @block.sync
        def _(sp):
            def load(u):
                sp.dma_start(raw[:, u % DEPTH, :], stream[u]).then_inc(raw_in[u % DEPTH], 16)

            xv = x_t.rearrange("(j k p) t -> j p k t", k=2, p=P)
            sp.dma_start(par[:, :], params).then_inc(par_in, 16)
            for j in range(KT // 2):
                if j < DEPTH:
                    load(j)
                sp.dma_start(hb[:, 2 * j:2 * j + 2, :], xv[j]).then_inc(x_in[j], 16)

            def load_loop(lo, hi):
                with sp.Fori(lo, hi) as i:
                    for s in range(DEPTH):
                        sp.wait_ge(lo_ready, DEPTH * i + (s + 1 - DEPTH))
                        src = stream[bass.ds(DEPTH * i + s, 1)].rearrange("o p n -> p (o n)")
                        sp.dma_start(raw[:, s, :], src).then_inc(raw_in[s], 16)

            turn = (U_OUT1 + 12) // DEPTH
            load_loop(1, turn)
            sp.wait_ge(xl_ready, XL_MIX + H)
            sp.wait_ge(pool_l, 2 * NT)
            for j in range(KT // 2):
                sp.dma_start(hb[:, 2 * j:2 * j + 2, :], xv[j]).then_inc(xr_in, 16)
            load_loop(turn, UNITS // DEPTH)
            ov = out_t.rearrange("(k p) t -> k p t", p=P)
            for m in STORE_ORDER:
                for done_, tiles in ((out_v, VECTOR_TILES), (out_g, POOL_TILES), (out_a, TENSOR_TILES)):
                    if m in tiles:
                        sp.wait_ge(done_, tiles.index(m) + 1)
                sp.dma_start(ov[m], hb[:, m, :]).then_inc(stored, 16)
            sp.wait_ge(stored, 16 * KT)

        @block.gpsimd
        def _(pool):
            pool.memset(ones[:, :], 1.0).then_inc(consts, 1)
            pool.memset(eps[:, :], EPS).then_inc(consts, 1)
            pool.memset(ident[:, :], 1.0).then_inc(pool_chain, 1)
            pool.memset(mask[:, :], 0.0).then_inc(pool_chain, 1)
            pool.wait_ge(pool_chain, 2)
            pool.affine_select(out=ident[:, :], in_=ident[:, :], compare_op=ALU.is_equal, fill=0.0,
                               base=0, pattern=[[-1, P]], channel_multiplier=1).then_inc(consts, 1)
            pool.affine_select(out=mask[:, :], in_=mask[:, :], compare_op=ALU.is_ge, fill=NEG,
                               base=0, pattern=[[1, P]], channel_multiplier=-1).then_inc(consts, 1)

            def low(i, s):
                pool.wait_ge(hi_ready, DEPTH * i + (s + 1))
                pool.tensor_tensor(wl[:, s, :], raw[:, s, :], wh[:, s, :].bitcast(F32),
                                   ALU.subtract).then_inc(lo_ready, 1)

            def low_loop(lo, hi):
                with pool.Fori(lo, hi) as i:
                    for s in range(DEPTH):
                        low(i, s)

            low_loop(0, UNITS // DEPTH)
            pool.wait_ge(row_ready, 4)
            for i, m in enumerate(POOL_TILES):
                pool.wait_ge(fin_g, m + 1)
                pool.tensor_tensor(acc[:, m, :], acc[:, m, :], row[:, :], ALU.mult).then_inc(pool_chain, 1)
                pool.wait_ge(pool_chain, 3 + i)
                pool.tensor_tensor(hb[:, m, :], hb[:, m, :], acc[:, m, :], ALU.add).then_inc(out_g, 1)

        @block.tensor
        def _(pe):
            held = {}

            def claim(g_, n):
                b = banks_of(g_) + n
                if b in held:
                    pe.wait_ge(tile_read, held[b] + 1)
                if g_ != G_EMB3:
                    held[b] = NT * g_ + n
                return bank[b]

            def three(out, a, b, first, last):
                pe.matmul(out, a[0], b[0], start=first, stop=False)
                pe.matmul(out, a[0], b[1], start=False, stop=False)
                return pe.matmul(out, a[1], b[0], start=False, stop=last)

            def weights(u, k, c0, c1):
                s = u % DEPTH
                return (wh[:, s, S * k + c0:S * k + c1], wl[:, s, S * k + c0:S * k + c1])

            def unit(u, g_, rhs, kts, need=None, first=True, last=True, tokens_out=False, inc=1,
                     busy=None):
                pe.wait_ge(lo_ready, u + 1)
                if need:
                    pe.wait_ge(need[0], need[1] + kts[1] + 1)
                for n in range(NT):
                    if busy and n == busy[0]:
                        pe.wait_ge(*busy[1:])
                    out = claim(g_, n) if first else bank[banks_of(g_) + n]
                    for k, kt in enumerate(kts):
                        x = (rhs[0][:, kt, :], rhs[1][:, kt, :])
                        st, en = first and k == 0, last and k == 1
                        if tokens_out:
                            x = tuple(v[:, n * P:(n + 1) * P] for v in x)
                            mm = three(out[:, :], x, weights(u, k, 0, S), st, en)
                        else:
                            mm = three(out[:, :], weights(u, k, n * P, (n + 1) * P), x, st, en)
                    mm.then_inc(pieces, inc if n == 0 else 1)

            X = (xh, xl)

            def keep_warm(b, n):
                for _ in range(n):
                    pe.matmul(bank[b][:, 0:P], ones[:, :], ones[:, :], start=True, stop=True)

            def early_unit(u, g_, kts, need, first, last, tokens_out=False):
                pe.wait_ge(lo_ready, u + 1)
                for k, kt in enumerate(kts):
                    pe.wait_ge(need[0], need[1] + kt + 1)
                    for n in range(NT):
                        out = claim(g_, n) if first and k == 0 else bank[banks_of(g_) + n]
                        st, en = first and k == 0, last and k == 1
                        if tokens_out:
                            x = (xh[:, kt, n * P:(n + 1) * P], xl[:, kt, n * P:(n + 1) * P])
                            mm = three(out[:, :], x, weights(u, k, 0, S), st, en)
                        else:
                            mm = three(out[:, :], weights(u, k, n * P, (n + 1) * P),
                                       (xh[:, kt, :], xl[:, kt, :]), st, en)
                        if k == 1:
                            mm.then_inc(pieces, 1)

            def group(u0, g_, need=None, tokens_out=False, after=None, busy=None):
                for j in range(KT // 2):
                    unit(u0 + j, g_, X, (2 * j, 2 * j + 1), need, j == 0, j == KT // 2 - 1, tokens_out,
                         busy=None if j else busy)
                    if after and j in after:
                        after[j]()

            def stat(b, src):
                pe.matmul(bank[b][:, :], ones[:, :], src[:, :], start=True, stop=True).then_inc(stat_mm, 1)

            def stat_and_last(b, src, base):
                pe.wait_ge(ss_ready, base[1] + KT - 2)
                pe.matmul(bank[b][:, :], ones[:, :], src[:, :], start=True, stop=False)
                for i in range(2):
                    pe.wait_ge(sq_ready, base[0] + KT - 1 + i)
                    mm = pe.matmul(bank[b][:, :], ones[:, :], tmp[:, i, :], start=False, stop=i == 1)
                mm.then_inc(stat_mm, 1)

            pe.wait_ge(consts, 4)
            keep_warm(7, 18)
            for j in range(7):
                early_unit(U_V0 + j, G_V0, (2 * j, 2 * j + 1), (xl_ready, 0), j == 0, False, True)
            pe.wait_ge(ss_ready, KT)
            for t in range(TT):
                pe.matmul(bank[5][:, 2 * t:2 * t + 2], ssq[:, t * P:(t + 1) * P], ones[:, 0:2],
                          start=True, stop=True)
            stat(4, ssq)
            unit(U_V0 + 7, G_V0, X, (14, 15), (xl_ready, 0), False, True, True)

            pe.wait_ge(lo_ready, U_GATES + 1)
            s = U_GATES % DEPTH
            for kt in range(KT):
                o = 2 * H * kt
                mm = three(bank[6][:, :], (wh[:, s, o:o + P], wl[:, s, o:o + P]),
                           (xh[:, kt, :], xl[:, kt, :]), kt == 0, kt == KT - 1)
            mm.then_inc(g_mm, 1)

            def forget_down():
                pe.wait_ge(g_sb, 1)
                pe.wait_ge(row_ready, 1)
                pe.matmul(bank[5][0:H, :], ident[0:2 * H, H:2 * H], dw[0:2 * H, 0:S],
                          start=True, stop=True).then_inc(g_tr, 1)

            def columns_across():
                pe.wait_ge(c_sb, 1)
                for i in range(BLOCKS + TT):
                    tr = pe.transpose(bank[6][:, H * i:H * (i + 1)], column_source(i), ident[0:H, 0:H])
                tr.then_inc(c_tr, 1)

            def column_source(i):
                if i < TT:
                    return tmp[0:H, 0, i * P:(i + 1) * P]
                if i < BLOCKS:
                    o = pair_at(i - TT)
                    return dw[0:H, o:o + P]
                return tmp[0:H, 1, (i - BLOCKS) * P:(i - BLOCKS + 1) * P]

            for j in range(8):
                unit(U_O0 + j, G_O0, X, (2 * j, 2 * j + 1), None, j == 0, j == 7, inc=5 if j == 0 else 1)
                if j == 1:
                    forget_down()
                if j == 5:
                    columns_across()
            group(U_Q0, G_Q0)
            group(U_K0, G_K0)

            def R(h):
                pe.wait_ge(sel_ready, h + 1)
                if h:
                    pe.wait_ge(d_ready, h)
                pe.matmul(bank[4][:, :], nsel[:, h % 2, :], ml, start=True, stop=True).then_inc(r_mm, 1)

            def scores(h):
                i, hl = h % HH, h % HH
                pe.wait_ge(qk_l, 8 * (h // HH + 1))
                if h:
                    pe.wait_ge(n_read, h)
                else:
                    pe.wait_ge(c_ready, 1)
                if h >= 2:
                    pe.wait_ge(cell_ready, h - (h % HH > 0))
                for j, o in SOURCES:
                    c = o % TT * P
                    k = (kh[:, hl, j * P:(j + 1) * P], kl[:, hl, j * P:(j + 1) * P])
                    q = (qh[:, hl, j * P:S], ql[:, hl, j * P:S])
                    mm = three(bank[5 + o // TT][:, c:c + (TT - j) * P], k, q, True, True)
                    if j != 1:
                        mm.then_inc(s_mm, 1)

            def cells(h):
                pe.wait_ge(p_l, 3 * (h + 1))
                if h % HH == 0:
                    pe.wait_ge(tile_read, NT * ((G_V1 if h else G_V0) + 1))
                for t in range(TT):
                    out = bank[5][:, 130 * t:130 * (t + 1)] if t < 3 else bank[6][:, 0:130]
                    for j in range(t + 1):
                        o = BLOCK[j, t] * P
                        mm = three(out, (ph[:, o:o + P], pl[:, o:o + P]),
                                   (vh[:, j, h % HH, :], vl[:, j, h % HH, :]), j == 0, j == t)
                mm.then_inc(n_mm, 1)

            def turn(h):
                pe.wait_ge(cn_ready, h + 1)
                pe.wait_ge(p_f, 3 * min(h + 2, HH * (h // HH + 1)))
                for t in range(TT):
                    tr = pe.transpose(bank[7][:, t * P:(t + 1) * P], cn[:, t * P:(t + 1) * P], ident[:, :])
                tr.then_inc(tr_mm, 1)

            def half(b, h0, u1, g1, u2, g2, tokens_out):
                steps = {2: lambda: R(h0)}
                for i in range(HH):
                    steps[3 + 2 * i] = lambda h=h0 + i, more=i + 1 < HH: (scores(h), R(h + 1) if more else None)
                    steps[4 + 2 * i] = lambda h=h0 + i, t=i > 0: (turn(h - 1) if t else None, cells(h))
                steps[4 + 2 * HH] = lambda: turn(h0 + HH - 1)
                group(u1, g1, after={j: f for j, f in steps.items() if j < 8})
                group(u2, g2, tokens_out=tokens_out, after={j - 8: f for j, f in steps.items() if j >= 8})

            half(0, 0, U_O1, G_O1, U_V1, G_V1, True)
            group(U_Q1, G_Q1)
            group(U_K1, G_K1)
            half(1, HH, U_U0, G_U0, U_U1, G_U1, False)

            def pool_unit(u, g_, src, need):
                pe.wait_ge(lo_ready, u + 1)
                pe.wait_ge(pool_l, need)
                s = u % DEPTH
                for n in range(NT):
                    out = claim(g_, n)
                    for k in range(2):
                        c = 512 * (n // 2) + 256 * k + P * (n % 2)
                        kt = 2 * (n // 2) + k
                        mm = three(out[:, :], (wh[:, s, c:c + P], wl[:, s, c:c + P]),
                                   (src[0][:, kt, :], src[1][:, kt, :]), k == 0, k == 1)
                    mm.then_inc(pieces, 1)

            pe.wait_ge(cell_ready, H)
            pool_unit(U_POOL0, G_POOL0, (qh, ql), NT)
            need = (xl_ready, XL_MIX)
            pooled = (tile_read, NT * G_POOL0 - H)
            for j in range(4):
                unit(U_OUT0A + j, G_OUT, X, (2 * j, 2 * j + 1), need, j == 0, False)
            pool_unit(U_POOL1, G_POOL1, (kh, kl), 2 * NT)
            for j in range(4):
                unit(U_OUT0B + j, G_OUT, X, (8 + 2 * j, 9 + 2 * j), pooled, False, j == 3)
            for i in range(3):
                group(U_OUT1 + 8 * i, G_OUT + 1 + i)
            pe.wait_ge(tile_read, NT * (G_OUT + 3))
            keep_warm(2, 5)
            stat_and_last(3, ssq, SQ_MIX)
            keep_warm(2, 18)
            pe.wait_ge(row_ready, 2)

            with pe.Fori(0, CHUNKS) as c:
                for k in range(2 + NT):
                    for j in range(8 if k < 2 else 4):
                        l = 8 * k + j if k < 2 else 16 + 4 * (k - 2) + j
                        s = (U_FF + l) % DEPTH
                        last = j == (7 if k < 2 else 3)
                        pe.wait_ge(lo_ready, FF_UNITS * c + (U_FF + l + 1))
                        src = X if k < 2 else (hidh, hidl)
                        if k == 1:
                            pe.wait_ge(xl_ready, XL_FF + 2 * j + 2)
                        elif k > 1:
                            pe.wait_ge(hid_l, HT * c + (2 * j + 2))
                        steps = [(kk, n) for kk in range(2) for n in range(NT)]
                        for kk, n in steps if k == 0 else sorted(steps, key=lambda step: step[1]):
                            if k == 0 and n == 0:
                                pe.wait_ge(xl_ready, XL_FF + 2 * j + kk + 1)
                            if j == 0 and kk == 0:
                                pe.wait_ge(tile_read, NT * 6 * c + (NT * (G_FF + k - 2) + n + 1))
                            kt = 2 * j + kk
                            o = S * kk + n * P
                            mm = three(bank[banks_of(G_FF + k) + n][:, :],
                                       (wh[:, s, o:o + P], wl[:, s, o:o + P]),
                                       (src[0][:, kt, :], src[1][:, kt, :]),
                                       j == 0 and kk == 0, last and kk == 1)
                            if kk == 1:
                                mm.then_inc(pieces, 1)
            for i in range(2):
                for n in range(NT):
                    held[banks_of(G_PLE - 2 + i) + n] = NT * (G_PLE - 2 + i) + n

            pe.wait_ge(tile_read, NT * (G_PLE - 1) + 3)
            pe.wait_ge(ss_ready, SQ_FF[1])
            stat(6, ssq)
            pe.wait_ge(p_copied, 2)
            for i in range(4):
                if i == 2:
                    pe.wait_ge(tile_read, NT * G_PLE)
                    stat_and_last(7, ssq2, SQ_FF)
                    pe.wait_ge(ffrow, 1)
                if i == 3:
                    pe.wait_ge(ffrow_v, 1)
                g_ = G_PLE + i if i < 3 else G_EMB3
                unit(U_PLE + i, g_, X, (KT - 2, KT - 1), None, True, True, inc=5 if i == 0 else 1,
                     busy=(3, ffrow_v, 1) if i == 2 else None)

            need = (xl_ready, XL_GATE)
            for j in range(KT // 2):
                early_unit(U_GATE + j, G_GATE, (2 * j, 2 * j + 1), need, j == 0, j == KT // 2 - 1)
            pe.wait_ge(emb_read, NT)
            pe.wait_ge(ss_ready, SQ_END[1])
            stat(3, ssq)
            for i in range(3):
                group(U_GATE + 8 * (i + 1), G_GATE + 1 + i, busy=None if i else (3, row_ready, 3))
            pe.wait_ge(tile_read, NT * (G_GATE + 3))
            def put_h(i):
                pe.matmul(bank[SUM_BANKS[i]][:, :], ident[:, :], hb[:, TENSOR_TILES[i], :],
                          start=True, stop=False)

            put_h(0)
            put_h(1)
            stat_and_last(4, ssq2, SQ_END)
            for i in range(2, len(TENSOR_TILES)):
                put_h(i)
            for i, m in enumerate(TENSOR_TILES):
                pe.wait_ge(y_scaled, i + 1)
                pe.matmul(bank[SUM_BANKS[i]][:, :], ident[:, :], acc[:, m, :], start=False,
                          stop=True).then_inc(sum_mm, 1)

        @block.scalar
        def _(act):
            link = linker(act, act_chain)

            def load_ln_exp():
                act.preload_act_table_set("natural_log_exp_and_others")

            def split(u):
                act.wait_ge(raw_in[u % DEPTH], 16 * (u // DEPTH + 1))
                if u >= DEPTH:
                    act.wait_ge(pieces, 4 * (u - DEPTH + 1))
                act.activation(wh[:, u % DEPTH, :], raw[:, u % DEPTH, :], ACT.Copy).then_inc(hi_ready, 1)

            def done(u, n):
                act.wait_ge(pieces, 4 * u + n + 1)

            def square(src, base, kt):
                if kt >= 2:
                    act.wait_ge(ss_ready, base[1] + kt - 1)
                act.activation(tmp[:, kt % 2, :], src, ACT.Square).then_inc(sq_ready, 1)

            def square_h(base, kt):
                if kt >= 2:
                    act.wait_ge(ss_ready, base[1] + max(kt - 2, 1))
                act.activation(tmp[:, kt % 2, :], hb[:, kt, :], ACT.Square).then_inc(sq_ready, 1)

            def inverse_rms(dst, src, n=1.0 / D):
                link(act.activation(dst, src, ACT.Ln, scale=n, bias=eps[:, :]))
                return act.activation(dst, dst, ACT.Exp, scale=-0.5)

            act.preload_act_table_set("exp_and_others")
            split(0)
            act.wait_ge(par_in, 16)
            for j in range(8):
                act.wait_ge(x_in[j], 16)
                for kt in (2 * j, 2 * j + 1):
                    act.activation(xh[:, kt, :], hb[:, kt, :], ACT.Copy,
                                   scale=g(C_MIX_PRE, kt)).then_inc(xh_ready, 1)
                if j:
                    split(j)
                for kt in (2 * j, 2 * j + 1):
                    square(hb[:, kt, :], SQ_X, kt)

            def stat_x():
                act.wait_ge(consts, 4)
                act.wait_ge(stat_mm, 1)
                link(inverse_rms(row[:, :], bank[4][:, :]))
                inverse_rms(tokf[:, :], bank[5][:, 0:2 * TT:2]).then_inc(row_ready, 1)

            def v_high(u):
                act.wait_ge(row_ready, 1)
                if u > U_V0 + 7:
                    act.wait_ge(n_mm, HH)
                for t in range(TT):
                    done(u, t)
                    act.activation(vh[:, t, :, 0:P], bank[t][:, :].rearrange("p (h d) -> p h d", h=HH),
                                   ACT.Copy, scale=tokf[:, t:t + 1]).then_inc(vh_ready, 1)

            def forget_ln():
                act.wait_ge(g_x, 1)
                link(act.activation(dw[0:H, 0:S], tmp[0:H, 1, :], ACT.Abs))
                link(act.activation(dw[0:H, 0:S], dw[0:H, 0:S], ACT.Exp, scale=-1.0))
                act.activation(dw[0:H, 0:S], dw[0:H, 0:S], ACT.Ln, bias=1.0).then_inc(g_ln, 1)

            def floor_exp():
                act.wait_ge(c_ready, 1)
                act.activation(colt[:, BLOCKS:, :], colt[:, BLOCKS:, :], ACT.Exp).then_inc(em_ready, 1)

            def sigmoid_o(b):
                for n in range(NT):
                    act.wait_ge(tile_read, NT * (G_O1 if b else G_O0) + n + 1)
                    act.activation(hb[:, HH * b + n, :], hb[:, HH * b + n, :], ACT.Sigmoid).then_inc(sig_ready, 1)

            def silu(i):
                dst = (qh, kh)[(i // NT) % 2]
                act.wait_ge(y_ready, i + 1)
                if i >= 2:
                    act.wait_ge(qk_l, i - 1)
                act.activation(tmp[:, i % 2, :], dw[:, S * (i % 2):S * (i % 2) + S], ACT.Silu).then_inc(qk_f, 1)
                act.wait_ge(qk_f, i + 1)
                act.activation(dst[:, i % NT, :], tmp[:, i % 2, :], ACT.Copy).then_inc(qk_h, 1)

            def exps(h):
                act.wait_ge(diag_ready, h + 1)
                for j in range(TT):
                    o = BLOCK[j, j] * P
                    act.activation(dw[:, o:o + P], dw[:, o:o + P], ACT.Exp, bias=colt[:, j, h:h + 1])
                for i, (j, t) in enumerate(OFF):
                    o = BLOCK[j, t] * P
                    e = act.activation(dw[:, o:o + P], bank[4][:, t * P:(t + 1) * P], ACT.Exp,
                                       bias=colt[:, TT + i, h:h + 1])
                e.then_inc(d_ready, 1)

            def p_high(h):
                for i, (a, b) in enumerate(P_PARTS):
                    act.wait_ge(p_f, 3 * h + i + 1)
                    if h:
                        act.wait_ge(n_mm, h)
                    act.activation(ph[:, a:b], dw[:, a:b], ACT.Copy).then_inc(p_h, 1)

            def cell_scale(h):
                act.wait_ge(cs_ready, h + 1)
                inverse_rms(crs[:, :], cssq[:, :], 1.0 / P).then_inc(cr_ready, 1)

            def pool_high(i):
                dst = (qh, kh)[i // NT]
                act.wait_ge(pool_f, i + 1)
                act.activation(dst[:, i % NT, :], tmp[:, i % 2, :], ACT.Copy).then_inc(pool_h, 1)

            def cell_high(kt):
                act.wait_ge(cell_ready, kt + 1)
                act.activation(xh[:, kt, :], hb[:, kt, :], ACT.Copy).then_inc(xh_ready, 1)

            def pooled_high(b, u):
                for n in range(NT):
                    done(u, n)
                    act.activation(xh[:, 8 + NT * b + n, :], bank[4 + n][:, :], ACT.Copy,
                                   scale=g(C_POOL, NT * b + n)).then_inc(xh_ready, 1)

            def mix_squares(i):
                for n in range(NT):
                    if (i, n) == (NT - 1, NT - 1):
                        done(U_FF - 1, n)
                        square(bank[banks_of(G_OUT + i) + n][:, :], SQ_MIX, NT * i + n)
                    else:
                        act.wait_ge(tile_read, NT * (G_OUT + i) + n + 1)
                        square(acc[:, NT * i + n, :], SQ_MIX, NT * i + n)

            def post_high(stage, kt, col):
                act.wait_ge(h_ready, KT * (stage - 2) + kt + 1)
                act.activation(xh[:, kt, :], hb[:, kt, :], ACT.Copy, scale=g(col, kt)).then_inc(xh_ready, 1)

            def row_stat(n_stat, dst, b):
                act.wait_ge(stat_mm, n_stat)
                return inverse_rms(dst, bank[b][:, :])

            during = {u: [] for u in range(UNITS)}
            before = {u: [] for u in range(UNITS)}

            def at(u, f, *args, first=False):
                (before if first else during)[u].append(lambda: f(*args))

            at(U_V0 + 6, stat_x)
            at(U_V0 + 7, v_high, U_V0 + 7)
            at(U_O0 + 2, forget_ln)
            at(U_O0 + 6, floor_exp)
            at(U_Q0, sigmoid_o, 0)
            for b, (uk, uo) in enumerate(((U_K0, U_O1), (U_K1, U_U0))):
                for n in range(NT):
                    at(uk + n, silu, 8 * b + n)
                for n in range(NT):
                    at(uo + n * 3 // 4, silu, 8 * b + NT + n)
                h0 = HH * b
                at(uo + 3, exps, h0)
                for i in range(HH):
                    at(uo + 4 + 2 * i, p_high, h0 + i)
                    if i + 1 < HH:
                        at(uo + 4 + 2 * i, exps, h0 + i + 1)
                    at(uo + 5 + 2 * i, cell_scale, h0 + i)
            at(U_O1 + 12, sigmoid_o, 1)
            at(U_V1 + 7, v_high, U_V1 + 7)
            for n in range(NT):
                at(U_U1 + 5 + n // 2, pool_high, n)
            for kt in range(H):
                at(U_POOL0, cell_high, kt, first=True)
            before[U_POOL0].insert(0, lambda: act.wait_ge(pieces, 4 * U_POOL0))
            at(U_POOL0, pooled_high, 0, U_POOL0)
            for n in range(NT):
                at(U_OUT0A + 1 + n // 2, pool_high, NT + n)
            at(U_POOL1, pooled_high, 1, U_POOL1)
            for i in range(3):
                at(U_OUT0B + 8 * i + 4, mix_squares, i)
            at(U_OUT1 + 23, mix_squares, 3)

            for u in range(5, U_FF):
                for f in before[u]:
                    f()
                split(u + LEAD)
                for f in during[u]:
                    f()

            load_ln_exp()
            split(U_FF + LEAD)
            row_stat(2, row[:, :], 3).then_inc(row_ready, 1)

            def h_tile(stage, kt):
                post_high(stage, kt, (C_FF_PRE, C_PLE_GATE)[stage - 2])
                square_h((SQ_H, SQ_G)[stage - 2], kt)

            def h_before(stage, j):
                post_high(stage, 2 * j + 1, (C_FF_PRE, C_PLE_GATE)[stage - 2])

            def h_after(stage, j):
                square_h((SQ_H, SQ_G)[stage - 2], 2 * j + 1)
                if 2 * j + 2 < KT:
                    h_tile(stage, 2 * j + 2)

            h_tile(2, 0)
            h_before(2, 0)
            h_after(2, 0)

            def hidden(c, j):
                t = HT * c + j
                act.wait_ge(tile_read, 6 * NT * c + (NT * G_FF + j + 1))
                r = tmp[:, j % 2, :]
                act.activation(r, r, ACT.Square).then_inc(ff_sq, 1)
                act.wait_ge(ff_sq, t + 1)
                act.activation(hidh[:, j, :], r, ACT.Copy).then_inc(hid_h, 1)

            def chunk(c, during, before=lambda l: None, start=0):
                for l in range(start, FF_UNITS):
                    u = U_FF + l + LEAD
                    before(l)
                    act.wait_ge(raw_in[u % DEPTH], 16 * FF_UNITS // DEPTH * c + 16 * (u // DEPTH + 1))
                    act.wait_ge(pieces, 4 * FF_UNITS * c + 4 * (u - DEPTH + 1))
                    act.activation(wh[:, u % DEPTH, :], raw[:, u % DEPTH, :], ACT.Copy).then_inc(hi_ready, 1)
                    if l in (8, 16):
                        for n in range(NT):
                            hidden(c, NT * (l // 8 - 1) + n)
                    during(l)

            def ff_squares(i):
                for n in range(NT):
                    act.wait_ge(tile_read, NT * (G_PLE - NT + i) + n + 1)
                    square(acc[:, NT * i + n, :], SQ_FF, NT * i + n)

            def last_chunk(l):
                if l in (20, 24, 28):
                    ff_squares(l // 4 - 5)

            chunk(0, lambda l: h_after(2, l) if l < 8 else None,
                  lambda l: h_before(2, l) if l < 8 else None, start=1)
            with act.Fori(1, CHUNKS - 1) as c:
                chunk(c, lambda l: None)
            chunk(CHUNKS - 1, last_chunk)

            ff_squares(NT - 1)
            load_ln_exp()
            split(U_P + LEAD)
            act.wait_ge(stat_mm, 3)
            act.activation(row[:, :], bank[6][:, :], ACT.Ln, scale=1.0 / D, bias=eps[:, :]).then_inc(ffrow, 1)
            act.wait_ge(ffrow, 1)
            act.activation(ssq[:, :], row[:, :], ACT.Exp, scale=-2.0).then_inc(ffrow, 1)
            split(U_PLE + LEAD)
            split(U_PLE + 1 + LEAD)
            act.wait_ge(ffrow_v, 1)
            act.activation(tmp[:, 1, :], tmp[:, 0, :], ACT.Ln, bias=eps[:, :]).then_inc(ffrow, 1)
            act.wait_ge(ffrow_v, 2)
            act.activation(row[:, :], tmp[:, 0, :], ACT.Exp, scale=-1.0).then_inc(ffrow, 1)
            split(U_PLE + 2 + LEAD)
            split(U_PLE + 3 + LEAD)

            def embedding_last(n):
                done(U_PLE + 3, n)
                act.activation(emb[:, 3 * NT + n, :], bank[n][:, :], ACT.Copy).then_inc(emb_read, 1)

            def sigmoid_gate(i, n):
                m = NT * i + n
                act.wait_ge(tile_read, NT * (G_GATE + i) + n + 1)
                act.activation(acc[:, m, :], acc[:, m, :], ACT.Sigmoid).then_inc(gsig, 1)

            def final_square(m):
                act.wait_ge(prod_ready, m + 1)
                square(acc[:, m, :], SQ_END, m)
                if m < KT - NT:
                    final_gain(m)

            def final_gain(m):
                act.activation(acc[:, m, :], acc[:, m, :], ACT.Copy, scale=g(C_PLE_POST, m)).then_inc(fin_g, 1)

            def gate_group(i):
                for n in range(NT):
                    sigmoid_gate(i, n)
                    if n:
                        final_square(NT * i + n - 1)
                final_square(NT * i + NT - 1)

            h_tile(3, 0)
            for u in range(U_GATE, UNITS):
                j = u - U_GATE
                if j < 8:
                    h_before(3, j)
                if u + LEAD < UNITS:
                    split(u + LEAD)
                if j < 8:
                    h_after(3, j)
                if 1 <= j <= NT:
                    embedding_last(j - 1)
                if j == 7:
                    load_ln_exp()
                if j == 8:
                    row_stat(5, row[:, :], 3).then_inc(row_ready, 1)
                if j in (9, 17, 25):
                    gate_group((j - 9) // 8)
            gate_group(3)
            load_ln_exp()
            row_stat(6, row[:, :], 4).then_inc(row_ready, 1)
            for m in range(KT - NT, KT):
                final_gain(m)
            for i, m in enumerate(TENSOR_TILES):
                act.wait_ge(sum_mm, i + 1)
                act.activation(hb[:, m, :], bank[SUM_BANKS[i]][:, :], ACT.Copy).then_inc(out_a, 1)

        @block.vector
        def _(dve):
            link = linker(dve, dve_chain)

            def done(u, n):
                dve.wait_ge(pieces, 4 * u + n + 1)

            def add_square(dst, base, kt):
                dve.wait_ge(sq_ready, base[0] + kt + 1)
                if kt == 0:
                    dve.tensor_copy(dst[:, :], tmp[:, 0, :]).then_inc(ss_ready, 1)
                else:
                    dve.wait_ge(ss_ready, base[1] + kt)
                    dve.tensor_tensor(dst[:, :], dst[:, :], tmp[:, kt % 2, :], ALU.add).then_inc(ss_ready, 1)

            link(*[dve.memset(vh[:, t, :, P:P + 1].bitcast(F32), 1.0) for t in range(TT)],
                 *[dve.memset(vh[:, t, :, P + 1:P + 2].bitcast(F32), 0.0) for t in range(TT)],
                 *[dve.memset(vl[:, t, :, P:P + 2].bitcast(F32), 0.0) for t in range(TT)],
                 *[dve.memset(win[:, t:t + 1], 1.0 / (t + 1)) for t in range(16)])

            dve.wait_ge(par_in, 16)
            for j in range(8):
                dve.wait_ge(x_in[j], 16)
                for kt in (2 * j, 2 * j + 1):
                    dve.wait_ge(xh_ready, kt + 1)
                    dve.scalar_tensor_tensor(out=xl[:, kt, :], in0=hb[:, kt, :], scalar=g(C_MIX_PRE, kt),
                                             in1=xh[:, kt, :].bitcast(F32), op0=ALU.mult,
                                             op1=ALU.subtract).then_inc(xl_ready, 1)
                for kt in (2 * j, 2 * j + 1):
                    add_square(ssq, SQ_X, kt)

            def v_low(b, u):
                for t in range(TT):
                    dve.wait_ge(vh_ready, NT * b + t + 1)
                    shape = bank[t][:, :].rearrange("p (h d) -> p h d", h=HH)
                    dve.scalar_tensor_tensor(out=vl[:, t, :, 0:P], in0=shape, scalar=tokf[:, t:t + 1],
                                             in1=vh[:, t, :, 0:P].bitcast(F32), op0=ALU.mult,
                                             op1=ALU.subtract).then_inc(tile_read, 1)

            def scaled(u, at_tile):
                for n in range(NT):
                    done(u, n)
                    dve.tensor_tensor(hb[:, at_tile + n, :], bank[n][:, :], row[:, :],
                                      ALU.mult).then_inc(tile_read, 1)

            v_low(0, U_V0 + 7)

            dve.wait_ge(g_mm, 1)
            dve.tensor_tensor(dw[0:2 * H, 0:S], bank[6][0:2 * H, :], row[0:2 * H, :], ALU.mult).then_inc(g_sb, 1)
            gi, fg = tmp[0:H, 0, :], tmp[0:H, 1, :]
            dve.wait_ge(g_sb, 1)
            link(dve.tensor_scalar(gi, dw[0:H, 0:S], par[0:H, C_BIAS:C_BIAS + 1], None, ALU.add))
            dve.wait_ge(g_tr, 1)
            dve.tensor_scalar(fg, bank[5][0:H, :], par[0:H, C_BIAS + 1:C_BIAS + 2], None,
                              ALU.add).then_inc(g_x, 1)
            dve.wait_ge(g_x, 1)
            dve.wait_ge(g_ln, 1)
            link(dve.scalar_tensor_tensor(out=fg, in0=fg, scalar=0.0, in1=dw[0:H, 0:S],
                                          op0=ALU.min, op1=ALU.subtract))
            bb = dw[0:H, S:2 * S]
            for t in range(TT):
                o = slice(t * P, (t + 1) * P)
                e = dve.tensor_tensor_scan(bb[:, o], ones[0:H, :], fg[:, o], 0.0, ALU.mult, ALU.add)
                link(e)
            link(dve.tensor_tensor(gi, gi, bb, ALU.subtract))
            for t in range(TT):
                o = slice(t * P, (t + 1) * P)
                link(dve.tensor_tensor_scan(ml[:, o], gi[:, o], gi[:, o], mp[:, t:t + 1] if t else 0.0,
                                            ALU.max, ALU.max))
                if t + 1 < TT:
                    e = (t + 1) * P
                    link(dve.tensor_tensor(mp[:, t + 1:t + 2], ml[:, e - 1:e], bb[:, e - 1:e], ALU.add))
            link(dve.tensor_tensor(fg, bb, ml, ALU.add))
            link(dve.tensor_scalar(fg, fg, -1.0, EXP_MAX, ALU.mult, ALU.min))
            for i, (j, t) in enumerate(OFF):
                o, e = pair_at(i), t * P
                src = gi[:, j * P:(j + 1) * P] if t == j + 1 else dw[0:H, pair_at(i - 1):pair_at(i - 1) + P]
                ins = dve.tensor_scalar(dw[0:H, o:o + P], src, bb[:, e - 1:e], None, ALU.add)
                if i + 1 < len(OFF):
                    link(ins)
            ins.then_inc(c_sb, 1)
            dve.wait_ge(c_tr, 1)
            dve.tensor_copy(colt[:, :, :], bank[6][:, 0:H * (BLOCKS + TT)].rearrange(
                "p (i h) -> p i h", h=H)).then_inc(c_ready, 1)

            scaled(U_O0 + 7, 0)

            def conv(i, tile, wtile):
                y = dw[:, S * (i % 2):S * (i % 2) + S]
                x = hb[:, tile, :]

                def w(k):
                    return par[:, C_CONV + CONV * wtile + k:C_CONV + CONV * wtile + k + 1]
                link(dve.tensor_scalar(y, x, w(CONV - 1), None, ALU.mult))
                for s in range(1, CONV):
                    ins = dve.scalar_tensor_tensor(out=y[:, s:], in0=x[:, :S - s], scalar=w(CONV - 1 - s),
                                                   in1=y[:, s:], op0=ALU.mult, op1=ALU.add)
                    if s < CONV - 1:
                        link(ins)
                ins.then_inc(y_ready, 1)

            def qk_low(i):
                dst, hi = ((ql, qh), (kl, kh))[(i // NT) % 2]
                dve.wait_ge(qk_h, i + 1)
                dve.tensor_tensor(dst[:, i % NT, :], tmp[:, i % 2, :], hi[:, i % NT, :].bitcast(F32),
                                  ALU.subtract).then_inc(qk_l, 1)

            def qk(b, is_k, u, g_):
                base = 8 + NT * is_k
                scaled(u + 7, base)
                dve.wait_ge(tile_read, NT * (g_ + 1))
                i0 = 8 * b + NT * is_k
                for n in range(NT):
                    conv(i0 + n, base + n, 8 * is_k + NT * b + n)
                    if n:
                        qk_low(i0 + n - 1)
                qk_low(i0 + NT - 1)

            def select(h):
                dve.tensor_scalar(nsel[:, h % 2, :], ones[0:H, :], ident[0:H, h:h + 1], -1.0,
                                  ALU.mult, ALU.mult).then_inc(sel_ready, 1)

            def diag(h):
                dve.wait_ge(r_mm, h + 1)
                if h % HH:
                    dve.wait_ge(p_l, 3 * h)
                for j in range(TT):
                    o = BLOCK[j, j] * P
                    e = dve.tensor_tensor(dw[:, o:o + P], bank[4][:, j * P:(j + 1) * P], mask[:, :], ALU.add)
                e.then_inc(diag_ready, 1)

            def weigh(h):
                dve.wait_ge(d_ready, h + 1)
                for i, (a, b) in enumerate(P_PARTS):
                    dve.wait_ge(s_mm, 3 * h + i + 1)
                    dve.scalar_tensor_tensor(out=dw[:, a:b], in0=bank[5 + i][:, 0:b - a], scalar=P ** -0.5,
                                             in1=dw[:, a:b], op0=ALU.mult, op1=ALU.mult).then_inc(p_f, 1)
                for i, (a, b) in enumerate(P_PARTS):
                    dve.wait_ge(p_h, 3 * h + i + 1)
                    dve.tensor_tensor(pl[:, a:b], dw[:, a:b], ph[:, a:b].bitcast(F32),
                                      ALU.subtract).then_inc(p_l, 1)

            def normalise(h):
                dve.wait_ge(n_mm, h + 1)
                dve.wait_ge(em_ready, 1)
                link(dve.tensor_copy(den[:, 0:3],
                                     bank[5][:, 0:390].rearrange("p (t n) -> p t n", n=130)[:, :, P]),
                     dve.tensor_copy(den[:, 3:4], bank[6][:, P:P + 1]))
                link(dve.scalar_tensor_tensor(out=den[:, :], in0=den[:, :], scalar=-1.0, in1=den[:, :],
                                              op0=ALU.mult, op1=ALU.max))
                link(dve.tensor_tensor(den[:, :], den[:, :], colt[:, BLOCKS:, h], ALU.max))
                link(dve.reciprocal(den[:, :], den[:, :]))
                for t in range(TT):
                    src = bank[5][:, 130 * t:130 * t + P] if t < 3 else bank[6][:, 0:P]
                    e = dve.tensor_scalar(cn[:, t * P:(t + 1) * P], src, den[:, t:t + 1], None, ALU.mult)
                e.then_inc(n_read, 1)
                dve.wait_ge(n_read, h + 1)
                for t in range(TT):
                    c = cn[:, t * P:(t + 1) * P]
                    e = dve.tensor_tensor_reduce(out=tmp[:, 1, t * P:(t + 1) * P], in0=c, in1=c, scale=1.0,
                                                 scalar=0.0, op0=ALU.mult, op1=ALU.add,
                                                 accum_out=cssq[:, t:t + 1])
                e.then_inc(cs_ready, 1)

            def scale_cell(h):
                dve.wait_ge(cr_ready, h + 1)
                for t in range(TT):
                    c = cn[:, t * P:(t + 1) * P]
                    e = dve.tensor_scalar(c, c, crs[:, t:t + 1], None, ALU.mult)
                e.then_inc(cn_ready, 1)

            def gate_cell(h):
                dve.wait_ge(tr_mm, h + 1)
                dve.wait_ge(sig_ready, h + 1)
                dve.scalar_tensor_tensor(out=hb[:, h, :], in0=bank[7][:, :], scalar=g(C_MLSTM, h),
                                         in1=hb[:, h, :], op0=ALU.mult, op1=ALU.mult).then_inc(cell_ready, 1)

            def half(h0, middle):
                select(h0)
                select(h0 + 1)
                diag(h0)
                for i in range(HH):
                    h = h0 + i
                    if i == 2:
                        middle()
                    if i:
                        scale_cell(h - 1)
                    weigh(h)
                    if i + 1 < HH:
                        diag(h + 1)
                        if i + 2 < HH:
                            select(h + 2)
                    if i:
                        gate_cell(h - 1)
                    normalise(h)
                scale_cell(h0 + HH - 1)
                gate_cell(h0 + HH - 1)

            qk(0, 0, U_Q0, G_Q0)
            qk(0, 1, U_K0, G_K0)
            half(0, lambda: scaled(U_O1 + 7, HH))
            v_low(1, U_V1 + 7)
            qk(1, 0, U_Q1, G_Q1)
            qk(1, 1, U_K1, G_K1)
            half(HH, lambda: scaled(U_U0 + 7, 8))

            def pooling(i):
                w = WINDOWS[i // 2]
                u = hb[:, 8 + i, :]
                src, d, flip = u, 1, 0
                if i:
                    dve.wait_ge(pool_f, i)
                while d < w:
                    dst = dw[:, S * flip:S * flip + S]
                    link(dve.tensor_copy(dst[:, 0:d], src[:, 0:d]),
                         dve.tensor_tensor(dst[:, d:], src[:, d:], src[:, :S - d], ALU.add))
                    src, d, flip = dst, 2 * d, 1 - flip
                out = tmp[:, i % 2, :]
                link(dve.tensor_tensor(out[:, 0:w - 1], src[:, 0:w - 1], win[:, 0:w - 1], ALU.mult))
                link(dve.tensor_tensor(out[:, 0:w - 1], out[:, 0:w - 1], u[:, 0:w - 1], ALU.subtract))
                dve.scalar_tensor_tensor(out=out[:, w - 1:], in0=src[:, w - 1:], scalar=1.0 / w,
                                         in1=u[:, w - 1:], op0=ALU.mult, op1=ALU.subtract).then_inc(pool_f, 1)

            def pool_low(i):
                dst, hi = ((ql, qh), (kl, kh))[i // NT]
                dve.wait_ge(pool_h, i + 1)
                dve.tensor_tensor(dst[:, i % NT, :], tmp[:, i % 2, :], hi[:, i % NT, :].bitcast(F32),
                                  ALU.subtract).then_inc(pool_l, 1)

            def pool_half(b):
                for n in range(NT):
                    pooling(NT * b + n)
                    if n:
                        pool_low(NT * b + n - 1)
                pool_low(NT * b + NT - 1)

            dve.wait_ge(tile_read, NT * (G_U0 + 1))
            pool_half(0)
            scaled(U_U1 + 7, 12)
            dve.wait_ge(cell_ready, H)
            for kt in range(H):
                dve.wait_ge(xh_ready, KT + kt + 1)
                dve.tensor_tensor(xl[:, kt, :], hb[:, kt, :], xh[:, kt, :].bitcast(F32),
                                  ALU.subtract).then_inc(xl_ready, 1)

            def pooled_low(b):
                for n in range(NT):
                    kt = 8 + NT * b + n
                    dve.wait_ge(xh_ready, KT + kt + 1)
                    dve.scalar_tensor_tensor(out=xl[:, kt, :], in0=bank[4 + n][:, :],
                                             scalar=g(C_POOL, NT * b + n), in1=xh[:, kt, :].bitcast(F32),
                                             op0=ALU.mult, op1=ALU.subtract).then_inc(tile_read, 1)

            pooled_low(0)
            dve.wait_ge(tile_read, NT * (G_POOL0 + 1))
            pool_half(1)
            pooled_low(1)

            for i in range(NT):
                u = U_OUT0B + 3 + 8 * i
                for n in range(NT):
                    if (i, n) == (NT - 1, NT - 1):
                        dve.wait_ge(sq_ready, SQ_MIX[0] + KT)
                    done(u, n)
                    dve.tensor_copy(acc[:, NT * i + n, :], bank[banks_of(G_OUT + i) + n][:, :])\
                       .then_inc(tile_read, 1)
                    if n and NT * i + n - 1 < KT - 2:
                        add_square(ssq, SQ_MIX, NT * i + n - 1)
                if i < NT - 1:
                    add_square(ssq, SQ_MIX, NT * i + NT - 1)

            def post_norm(stage, post, pre, base, between=None):
                def low(kt):
                    dve.wait_ge(xh_ready, KT * stage + kt + 1)
                    dve.scalar_tensor_tensor(out=xl[:, kt, :], in0=hb[:, kt, :], scalar=g(pre, kt),
                                             in1=xh[:, kt, :].bitcast(F32), op0=ALU.mult,
                                             op1=ALU.subtract).then_inc(xl_ready, 1)

                def scale(kt):
                    dve.tensor_tensor(acc[:, kt, :], acc[:, kt, :], row[:, :], ALU.mult).then_inc(scaled_acc, 1)

                def add(kt):
                    dve.wait_ge(sq_ready, base[0] + kt + 1)
                    if kt > 1:
                        dve.wait_ge(ss_ready, base[1] + kt - 1)
                    dve.tensor_tensor(ssq[:, :], ssq[:, :] if kt > 1 else tmp[:, 0, :], tmp[:, kt % 2, :],
                                      ALU.add).then_inc(ss_ready, 1)

                scale(0)
                for kt in range(KT):
                    if between:
                        between(kt)
                    dve.wait_ge(scaled_acc, KT * (stage - 2) + kt + 1)
                    dve.scalar_tensor_tensor(out=hb[:, kt, :], in0=acc[:, kt, :], scalar=g(post, kt),
                                             in1=hb[:, kt, :], op0=ALU.mult, op1=ALU.add).then_inc(h_ready, 1)
                    if kt + 1 < KT:
                        scale(kt + 1)
                    if kt >= 2:
                        add(kt - 1)
                    low(kt)
                add(KT - 1)

            dve.wait_ge(row_ready, 2)
            dve.wait_ge(xr_in, 16 * KT // 2)
            dve.wait_ge(tile_read, NT * G_FF)
            post_norm(2, C_MIX_POST, C_FF_PRE, SQ_H)
            link(dve.memset(acc[:, :, :], 0.0))

            def chunk(c, last=False):
                def low(j):
                    dve.wait_ge(hid_h, HT * c + (j + 1))
                    dve.tensor_tensor(hidl[:, j, :], tmp[:, j % 2, :], hidh[:, j, :].bitcast(F32),
                                      ALU.subtract).then_inc(hid_l, 1)
                for k in range(2 + NT):
                    u = U_FF + (8 * k + 7 if k < 2 else 16 + 4 * (k - 2) + 3)
                    if last and k == 5:
                        copy_p()
                    for n in range(NT):
                        b = bank[banks_of(G_FF + k) + n]
                        dve.wait_ge(pieces, 4 * FF_UNITS * c + (4 * u + n + 1))
                        if k < 2:
                            j = NT * k + n
                            if j >= 2:
                                dve.wait_ge(hid_l, HT * c + (j - 1))
                            dve.tensor_scalar(tmp[:, j % 2, :], b[:, :], 0.0, None, ALU.max)\
                               .then_inc(tile_read, 1)
                            if j:
                                low(j - 1)
                            if j == HT - 1:
                                low(j)
                        else:
                            m = NT * (k - 2) + n
                            dve.tensor_tensor(acc[:, m, :], b[:, :], acc[:, m, :], ALU.add)\
                               .then_inc(tile_read, 1)
                            if last and n and m - 1 < KT - 2:
                                add_square(ssq2, SQ_FF, m - 1)
                    if last and 2 <= k < 5:
                        add_square(ssq2, SQ_FF, NT * (k - 2) + NT - 1)

            def copy_p():
                dve.wait_ge(lo_ready, U_P + 1)
                s = U_P % DEPTH
                dve.tensor_copy(xh[:, KT - 2:, :], wh[:, s, :].bitcast(F32).rearrange(
                    "p (k t) -> p k t", k=2)).then_inc(p_copied, 1)
                dve.tensor_copy(xl[:, KT - 2:, :], wl[:, s, :].bitcast(F32).rearrange(
                    "p (k t) -> p k t", k=2)).then_inc(p_copied, 1)

            with dve.Fori(0, CHUNKS - 1) as c:
                chunk(c)
            chunk(CHUNKS - 1, last=True)

            def embedding(i):
                for n in range(NT):
                    done(U_PLE + i, n)
                    dve.tensor_copy(emb[:, NT * i + n, :], bank[banks_of(G_PLE + i) + n][:, :])\
                       .then_inc(tile_read, 1)

            embedding(0)
            embedding(1)
            dve.wait_ge(ffrow, 2)
            dve.wait_ge(stat_mm, 4)
            dve.scalar_tensor_tensor(out=tmp[:, 0, :], in0=bank[7][:, :], scalar=1.0 / D, in1=ssq[:, :],
                                     op0=ALU.mult, op1=ALU.mult).then_inc(ffrow_v, 1)
            dve.wait_ge(ffrow, 3)
            dve.scalar_tensor_tensor(out=tmp[:, 0, :], in0=tmp[:, 1, :], scalar=0.5, in1=row[:, :],
                                     op0=ALU.mult, op1=ALU.add).then_inc(ffrow_v, 1)
            dve.wait_ge(ffrow, 4)
            post_norm(3, C_FF_POST, C_PLE_GATE, SQ_G,
                      between=lambda kt: embedding(2) if kt == 1 else None)

            dve.wait_ge(row_ready, 3)
            for i in range(NT):
                def product(m):
                    dve.wait_ge(gsig, m + 1)
                    dve.tensor_tensor(acc[:, m, :], acc[:, m, :], emb[:, m, :], ALU.mult)\
                       .then_inc(prod_ready, 1)
                for n in range(NT + 2):
                    m = NT * i + n
                    if n < NT:
                        done(U_GATE + 8 * i + 7, n)
                        dve.tensor_tensor(acc[:, m, :], bank[banks_of(G_GATE + i) + n][:, :], row[:, :],
                                          ALU.mult).then_inc(tile_read, 1)
                    if 1 <= n <= NT:
                        product(m - 1)
                    if n >= 2 and m - 2 < KT - 2:
                        add_square(ssq2, SQ_END, m - 2)
            dve.wait_ge(row_ready, 4)

            def add_up(m):
                i = VECTOR_TILES.index(m)
                dve.wait_ge(scaled_acc, 2 * KT + i + 1)
                dve.tensor_tensor(hb[:, m, :], hb[:, m, :], acc[:, m, :], ALU.add).then_inc(out_v, 1)

            scaled_last = None
            for m in VECTOR_ORDER:
                own = m in VECTOR_TILES
                dve.wait_ge(fin_g, m + 1)
                dve.tensor_tensor(acc[:, m, :], acc[:, m, :], row[:, :], ALU.mult)\
                   .then_inc(scaled_acc if own else y_scaled, 1)
                if scaled_last is not None:
                    add_up(scaled_last)
                scaled_last = m if own else None
                if m == VECTOR_ORDER[0]:
                    add_up(m)
                    scaled_last = None
            add_up(scaled_last)


def pair_at(i):
    return i * P if i < 4 else 2 * S + (i - 4) * P


P_PARTS = [(0, S), (S, 2 * S), (2 * S, BLOCKS * P)]
POOL_TILES = [1, 4, 7, 10]
VECTOR_TILES = [0, 3, 6, 9, 12, 13, 15]
TENSOR_TILES = [2, 5, 8, 11, 14]
SUM_BANKS = [5, 6, 7, 0, 1]
VECTOR_ORDER = [0, 2, 3, 5, 6, 8, 9, 11, 12, 14, 13, 15]
STORE_ORDER = [0, 1, 2, 3, 5, 4, 6, 8, 9, 7, 11, 12, 14, 10, 13, 15]


def pack(w):
    k, n = w.shape
    return w.reshape(k // 256, 2, P, n // 512, 512).transpose(3, 0, 2, 1, 4).reshape(
        n // 512, k // 256, P, 1024)


def kernel(x, p, w_in, b_gates, w_qk_conv, g_mlstm, w_pool, pool_scale, w_out, g_mix_pre, g_mix_post,
           w_ff1, w_ff2, g_ff_pre, g_ff_post, w_ple_proj, w_ple_gate, g_ple_gate, g_ple_post):
    import numpy as np
    import concourse.bacc as bacc
    from concourse.bass_utils import run_bass_kernel_spmd

    a = {k: np.asarray(v)[0] for k, v in dict(
        x=x, p=np.asarray(p)[0], w_in=w_in, b_gates=b_gates, conv=w_qk_conv, g_mlstm=g_mlstm,
        w_pool=w_pool, pool_scale=pool_scale, w_out=w_out, g_mix_pre=g_mix_pre, g_mix_post=g_mix_post,
        w_ff1=w_ff1, w_ff2=w_ff2, g_ff_pre=g_ff_pre, g_ff_post=g_ff_post, w_ple_proj=w_ple_proj,
        w_ple_gate=w_ple_gate, g_ple_gate=g_ple_gate, g_ple_post=g_ple_post).items()}
    w = a["w_in"]
    m = D // 2
    q, k, v, o = (pack(w[:, i * m:(i + 1) * m]) for i in range(4))
    gates = w[:, 4 * m:4 * m + 2 * H]
    u = pack(w[:, 4 * m + 2 * H:])
    gates_u = np.zeros((1, P, 1024), np.float32)
    gates_u[0, :, 0:KT * 2 * H] = gates.reshape(KT, P, 2 * H).transpose(1, 0, 2).reshape(P, -1)
    pools = a["w_pool"].reshape(2, 2, 2, P, 256).transpose(0, 3, 1, 2, 4).reshape(2, P, 1024)
    wo = pack(a["w_out"])
    ff1 = pack(a["w_ff1"]).reshape(CHUNKS, 16, P, 1024)
    ff2 = pack(a["w_ff2"]).reshape(4, CHUNKS, 4, P, 1024).transpose(1, 0, 2, 3, 4).reshape(
        CHUNKS, 16, P, 1024)
    ff = np.concatenate([ff1, ff2], axis=1).reshape(-1, P, 1024)
    p_unit = a["p"].T.reshape(2, P, S).transpose(1, 0, 2).reshape(1, P, 1024)
    stream = np.concatenate([
        v[0], gates_u, o[0], q[0], k[0], o[1], v[1], q[1], k[1], u[0], u[1], pools[0:1], wo[0, 0:4],
        pools[1:2], wo[0, 4:8], wo[1], wo[2], wo[3], ff, p_unit,
        pack(a["w_ple_proj"]).reshape(4, P, 1024), pack(a["w_ple_gate"]).reshape(32, P, 1024)])
    assert stream.shape[0] == UNITS
    par = np.zeros((P, PARAMS), np.float32)
    for c, name in ((C_MIX_PRE, "g_mix_pre"), (C_MIX_POST, "g_mix_post"), (C_FF_PRE, "g_ff_pre"),
                    (C_FF_POST, "g_ff_post"), (C_PLE_GATE, "g_ple_gate"), (C_PLE_POST, "g_ple_post"),
                    (C_MLSTM, "g_mlstm"), (C_POOL, "pool_scale")):
        t = a[name].reshape(-1, P).T
        par[:, c:c + t.shape[1]] = t
    par[:, C_CONV:C_CONV + 16 * CONV] = a["conv"].reshape(CONV, 16, P).transpose(2, 1, 0).reshape(P, -1)
    par[0:H, C_BIAS:C_BIAS + 2] = a["b_gates"].reshape(2, H).T
    arrays = {"stream": np.ascontiguousarray(stream), "x_t": np.ascontiguousarray(a["x"].T), "params": par}

    nc = bacc.Bacc("TRN2", target_bir_lowering=False, num_devices=1, dynamic_dma_scratch_size=1024)
    aps = [nc.dram_tensor(n, arr.shape, F32, kind="ExternalInput").ap() for n, arr in arrays.items()]
    out = nc.dram_tensor("out_t", (D, S), F32, kind="ExternalOutput").ap()
    build(nc, *aps, out)
    r = run_bass_kernel_spmd(nc, [arrays], core_ids=[0])
    return np.ascontiguousarray(r.results[0]["out_t"].T)[None]
```
